# Optimizing a Trainium2 kernel written in Bass

```python
import jax, jax.numpy as jnp
from jax import lax
import numpy as np
import math
import jax
import jax.numpy as jnp

D_MODEL = 1024
BATCH = 1
SEQ = 512
DEPTH = 1

GLA_HEADS = 4
GLA_DK = 128
GLA_DV = 128
GLA_RANK = 16
GLA_TAU = 16.0
GLA_CHUNK = 64
CONV_CH = D_MODEL // 2
CONV_K = 3
SWA_Q_HEADS = 8
SWA_KV_HEADS = 2
SWA_HEAD_DIM = 64
SWA_WINDOW = 128
D_FF = 2816
FFN_CONV_K = 3
N_BRANCH = 3
EPS = 1e-6

MIX_SIZES = (
    GLA_HEADS * GLA_DK,
    GLA_HEADS * GLA_DK,
    GLA_HEADS * GLA_DV,
    GLA_HEADS * GLA_DV,
    GLA_RANK,
    CONV_CH,
    CONV_CH,
    CONV_CH,
    SWA_Q_HEADS * SWA_HEAD_DIM,
    SWA_KV_HEADS * SWA_HEAD_DIM,
    SWA_KV_HEADS * SWA_HEAD_DIM,
    N_BRANCH * D_MODEL,
)
D_IN_TOTAL = sum(MIX_SIZES)


def rmsnorm(x, g):
    xf = x.astype(jnp.float32)
    y = xf * lax.rsqrt(jnp.mean(xf * xf, axis=-1, keepdims=True) + EPS)
    return (y * g.astype(jnp.float32)).astype(x.dtype)

def split_columns(z):
    out = []
    off = 0
    for n in MIX_SIZES:
        out.append(z[..., off:off + n])
        off += n
    return out

def causal_dwconv(u, w):
    K = w.shape[0]
    S = u.shape[1]
    up = jnp.pad(u, ((0, 0), (K - 1, 0), (0, 0)))
    y = up[:, 0:S] * w[0]
    for i in range(1, K):
        y = y + up[:, i:i + S] * w[i]
    return y

def alibi_slopes(n_heads):
    return jnp.exp2(-(8.0 / n_heads) * jnp.arange(1, n_heads + 1, dtype=jnp.float32))

def gla_chunked(q, k, v, log_a):
    f32 = jnp.float32
    Bsz, S, H, dk = q.shape
    dv = v.shape[-1]
    C = GLA_CHUNK
    N = S // C
    q = (q.astype(f32) * dk ** -0.5).reshape(Bsz, N, C, H, dk)
    k = k.astype(f32).reshape(Bsz, N, C, H, dk)
    v = v.astype(f32).reshape(Bsz, N, C, H, dv)
    b = jnp.cumsum(log_a.astype(f32).reshape(Bsz, N, C, H, dk), axis=2)
    b_ref = b[:, :, C // 2 - 1:C // 2]
    b_last = b[:, :, C - 1:]
    causal = jnp.tril(jnp.ones((C, C), dtype=bool))
    attn = jnp.einsum('bnihk,bnjhk->bnhij', q * jnp.exp(b - b_ref), k * jnp.exp(b_ref - b))
    attn = jnp.where(causal, attn, 0.0)
    o_intra = jnp.einsum('bnhij,bnjhv->bnihv', attn, v)
    kv = jnp.einsum('bnjhk,bnjhv->bnhkv', k * jnp.exp(b_last - b), v)
    decay = jnp.exp(b_last[:, :, 0])

    def step(state, inp):
        d, kv_n = inp
        return d[..., None] * state + kv_n, state

    s0 = jnp.zeros((Bsz, H, dk, dv), f32)
    _, s_prev = lax.scan(step, s0, (jnp.moveaxis(decay, 1, 0), jnp.moveaxis(kv, 1, 0)))
    s_prev = jnp.moveaxis(s_prev, 0, 1)
    o_inter = jnp.einsum('bnihk,bnhkv->bnihv', q * jnp.exp(b), s_prev)
    return (o_intra + o_inter).reshape(Bsz, S, H, dv)

def swa_sink_attention(q, k, v, sinks, slopes):
    f32 = jnp.float32
    Bsz, S, Hq, hd = q.shape
    Hkv = k.shape[2]
    G = Hq // Hkv
    W = SWA_WINDOW
    Nb = S // W
    qb = (q.astype(f32) * hd ** -0.5).reshape(Bsz, Nb, W, Hkv, G, hd)

    def windows(t):
        tp = jnp.pad(t.astype(f32), ((0, 0), (W, 0), (0, 0), (0, 0))).reshape(Bsz, Nb + 1, W, Hkv, hd)
        return jnp.concatenate([tp[:, :-1], tp[:, 1:]], axis=2)

    kw = windows(k)
    vw = windows(v)
    scores = jnp.einsum('bnqhgd,bnkhd->bnhgqk', qb, kw)
    iq = jnp.arange(W)[:, None]
    jk = jnp.arange(2 * W)[None, :]
    dist = W + iq - jk
    blk = jnp.arange(Nb)[:, None, None]
    valid = (dist >= 0) & (dist < W) & (blk * W - W + jk >= 0)
    alibi = -slopes.reshape(Hkv, G)[:, :, None, None] * dist.astype(f32)
    logits = jnp.where(valid[None, :, None, None], scores + alibi, -jnp.inf)
    sink = sinks.astype(f32).reshape(Hkv, G)[None, None, :, :, None]
    m = jnp.maximum(logits.max(axis=-1), sink)
    p = jnp.exp(logits - m[..., None])
    denom = p.sum(axis=-1) + jnp.exp(sink - m)
    o = jnp.einsum('bnhgqk,bnkhd->bnqhgd', p, vw) / jnp.moveaxis(denom, 4, 2)[..., None]
    return o.reshape(Bsz, S, Hq * hd)

def first_inputs(seed: int = 0) -> dict:
    key = jax.random.key(seed)
    ks = jax.random.split(key, 17)
    f32 = jnp.float32

    def nrm(k, shape, scale):
        return jax.random.normal(k, shape, f32) * scale

    return {
        'x': nrm(ks[0], (BATCH, SEQ, D_MODEL), 1.0),
        'g_mix': 1.0 + nrm(ks[1], (DEPTH, D_MODEL), 0.02),
        'w_in': nrm(ks[2], (DEPTH, D_MODEL, D_IN_TOTAL), D_MODEL ** -0.5),
        'gla_w_alpha': nrm(ks[3], (DEPTH, GLA_RANK, GLA_HEADS * GLA_DK), GLA_RANK ** -0.5),
        'gla_b_alpha': nrm(ks[4], (DEPTH, GLA_HEADS * GLA_DK), 0.02),
        'gla_norm_g': 1.0 + nrm(ks[5], (DEPTH, GLA_HEADS * GLA_DV), 0.02),
        'conv_w': nrm(ks[6], (DEPTH, CONV_K, CONV_CH), CONV_K ** -0.5),
        'swa_sinks': nrm(ks[7], (DEPTH, SWA_Q_HEADS), 0.5),
        'w_gla_o': nrm(ks[8], (DEPTH, GLA_HEADS * GLA_DV, D_MODEL), (GLA_HEADS * GLA_DV) ** -0.5),
        'w_conv_o': nrm(ks[9], (DEPTH, CONV_CH, D_MODEL), CONV_CH ** -0.5),
        'w_swa_o': nrm(ks[10], (DEPTH, SWA_Q_HEADS * SWA_HEAD_DIM, D_MODEL), (SWA_Q_HEADS * SWA_HEAD_DIM) ** -0.5),
        'w_o': nrm(ks[11], (DEPTH, D_MODEL, D_MODEL), D_MODEL ** -0.5),
        'g_ffn': 1.0 + nrm(ks[12], (DEPTH, D_MODEL), 0.02),
        'w_up': nrm(ks[13], (DEPTH, D_MODEL, 2 * D_FF), D_MODEL ** -0.5),
        'ffn_conv_w': nrm(ks[14], (DEPTH, FFN_CONV_K, 2 * D_FF), FFN_CONV_K ** -0.5),
        'w_down': nrm(ks[15], (DEPTH, D_FF, D_MODEL), D_FF ** -0.5),
        'g_final': 1.0 + nrm(ks[16], (D_MODEL,), 0.02),
    }

def first_block(x, g_mix, w_in, gla_w_alpha, gla_b_alpha, gla_norm_g, conv_w, swa_sinks, w_gla_o, w_conv_o, w_swa_o, w_o, g_ffn, w_up, ffn_conv_w, w_down, g_final):
    f32 = jnp.float32
    Bsz, S, _ = x.shape
    slopes = alibi_slopes(SWA_Q_HEADS)
    h = x
    for l in range(DEPTH):
        u = rmsnorm(h, g_mix[l])
        z = u @ w_in[l]
        gq, gk, gv, gr, ga, cx, cb, cc, sq, sk, sv, gates = split_columns(z)

        log_a = jax.nn.log_sigmoid((ga @ gla_w_alpha[l] + gla_b_alpha[l]).astype(f32)) / GLA_TAU
        o = gla_chunked(gq.reshape(Bsz, S, GLA_HEADS, GLA_DK),
                        gk.reshape(Bsz, S, GLA_HEADS, GLA_DK),
                        gv.reshape(Bsz, S, GLA_HEADS, GLA_DV),
                        log_a.reshape(Bsz, S, GLA_HEADS, GLA_DK))
        o = o * lax.rsqrt(jnp.mean(o * o, axis=-1, keepdims=True) + EPS)
        o = o.reshape(Bsz, S, GLA_HEADS * GLA_DV) * gla_norm_g[l].astype(f32)
        y_gla = (o * jax.nn.silu(gr.astype(f32))).astype(x.dtype) @ w_gla_o[l]

        y_conv = (cb * causal_dwconv(cc * cx, conv_w[l])) @ w_conv_o[l]

        o = swa_sink_attention(sq.reshape(Bsz, S, SWA_Q_HEADS, SWA_HEAD_DIM),
                               sk.reshape(Bsz, S, SWA_KV_HEADS, SWA_HEAD_DIM),
                               sv.reshape(Bsz, S, SWA_KV_HEADS, SWA_HEAD_DIM),
                               swa_sinks[l], slopes)
        y_swa = o.astype(x.dtype) @ w_swa_o[l]

        gt = jax.nn.sigmoid(gates)
        merged = (gt[..., :D_MODEL] * y_gla
                  + gt[..., D_MODEL:2 * D_MODEL] * y_conv
                  + gt[..., 2 * D_MODEL:] * y_swa)
        h = h + merged @ w_o[l]

        u = rmsnorm(h, g_ffn[l])
        hid = causal_dwconv(u @ w_up[l], ffn_conv_w[l])
        h = h + (jax.nn.silu(hid[..., :D_FF]) * hid[..., D_FF:]) @ w_down[l]
    return rmsnorm(h, g_final)


N_META = 16
D_MIX = 2 * D_MODEL
HG_WIDTH = D_MIX // 2
HG_DK = 128
HG_HEADS = HG_WIDTH // 128
HG_DV = HG_WIDTH // HG_HEADS
HG_KEY = HG_HEADS * HG_DK
HG_CHUNK = 16
M2_WIDTH = D_MIX - HG_WIDTH
M2_HEADDIM = 64
M2_HEADS = M2_WIDTH // M2_HEADDIM
M2_STATE = 128
M2_GROUPS = 2
M2_HPG = M2_HEADS // M2_GROUPS
M2_GN = M2_GROUPS * M2_STATE
M2_XBC = M2_WIDTH + 2 * M2_GN
M2_CONV = 4
M2_CHUNK = 64
DT_MIN = 1e-3
DT_MAX = 1e-1
FFN_CONV = 3
PROJ_SIZES = (HG_KEY, HG_KEY, HG_WIDTH, HG_WIDTH, M2_WIDTH, M2_XBC, M2_HEADS)
D_PROJ = sum(PROJ_SIZES)
PROJ_SPLITS = tuple(int(v) for v in np.cumsum(PROJ_SIZES)[:-1])


def rmsnorm_2(x, w):
    xf = x.astype(jnp.float32)
    y = xf * lax.rsqrt(jnp.mean(xf * xf, axis=-1, keepdims=True) + EPS)
    return (y * w.astype(jnp.float32)).astype(x.dtype)

def causal_dwconv_2(x, w, b):
    k_taps, length = w.shape[0], x.shape[1]
    xp = jnp.pad(x, ((0, 0), (k_taps - 1, 0), (0, 0)))
    y = b + xp[:, 0:length] * w[0]
    for k in range(1, k_taps):
        y = y + xp[:, k:k + length] * w[k]
    return y

def front_pad(t, n):
    return jnp.pad(t, ((0, 0), (n, 0)) + ((0, 0),) * (t.ndim - 2))

def to_chunks(t, c):
    return t.reshape((t.shape[0], t.shape[1] // c, c) + t.shape[2:])

def hgrn2_mixer(q, f_pre, i_in, g, lb, norm_w):
    bsz, length, _ = q.shape
    f32 = jnp.float32
    f = lb + (1.0 - lb) * jax.nn.sigmoid(f_pre.astype(f32))
    k = 1.0 - f
    log_f = jnp.log(f)
    qa = jax.nn.silu(q.astype(f32))
    pad = (-N_META) % HG_CHUNK
    lp = length + pad

    def prep(t, d):
        return to_chunks(front_pad(t, pad).reshape(bsz, lp, HG_HEADS, d), HG_CHUNK)

    qc, kc, gc = prep(qa, HG_DK), prep(k, HG_DK), prep(log_f, HG_DK)
    vc = prep(i_in.astype(f32), HG_DV)
    bcum = jnp.cumsum(gc, axis=2)
    blast = bcum[:, :, -1]
    q_dec = qc * jnp.exp(bcum)
    k_inv = kc * jnp.exp(-bcum)
    k_end = kc * jnp.exp(blast[:, :, None] - bcum)
    causal = jnp.tril(jnp.ones((HG_CHUNK, HG_CHUNK), dtype=bool))
    scores = jnp.einsum('bnrhk,bnshk->bnhrs', q_dec, k_inv)
    scores = jnp.where(causal, scores, 0.0)
    o_intra = jnp.einsum('bnhrs,bnshv->bnrhv', scores, vc)

    def step(state, inp):
        q_n, k_n, v_n, d_n = inp
        o_n = jnp.einsum('brhk,bhkv->brhv', q_n, state)
        state = d_n[..., None] * state + jnp.einsum('brhk,brhv->bhkv', k_n, v_n)
        return state, o_n

    s0 = jnp.zeros((bsz, HG_HEADS, HG_DK, HG_DV), f32)
    xs = (jnp.moveaxis(q_dec, 1, 0), jnp.moveaxis(k_end, 1, 0),
          jnp.moveaxis(vc, 1, 0), jnp.moveaxis(jnp.exp(blast), 1, 0))
    _, o_inter = lax.scan(step, s0, xs)
    o = o_intra + jnp.moveaxis(o_inter, 0, 1)
    o = o.reshape(bsz, lp, HG_HEADS, HG_DV)[:, pad:]
    o = o * lax.rsqrt(jnp.mean(o * o, axis=-1, keepdims=True) + EPS)
    o = o.reshape(bsz, length, HG_WIDTH) * norm_w.astype(f32)
    return (o * jax.nn.silu(g.astype(f32))).astype(q.dtype)

def mamba2_mixer(z, xbc, dt_pre, conv_w, conv_b, dt_bias, a_log, d_skip, norm_w):
    bsz, length, _ = z.shape
    f32 = jnp.float32
    xbc = jax.nn.silu(causal_dwconv_2(xbc, conv_w, conv_b).astype(f32))
    x_in = xbc[..., :M2_WIDTH].reshape(bsz, length, M2_GROUPS, M2_HPG, M2_HEADDIM)
    b_in = xbc[..., M2_WIDTH:M2_WIDTH + M2_GN].reshape(bsz, length, M2_GROUPS, M2_STATE)
    c_in = xbc[..., M2_WIDTH + M2_GN:].reshape(bsz, length, M2_GROUPS, M2_STATE)
    dt = jax.nn.softplus(dt_pre.astype(f32) + dt_bias.astype(f32))
    dt = dt.reshape(bsz, length, M2_GROUPS, M2_HPG)
    a = -jnp.exp(a_log.astype(f32)).reshape(M2_GROUPS, M2_HPG)
    da = dt * a
    xdt = x_in * dt[..., None]
    pad = (-N_META) % M2_CHUNK
    lp = length + pad
    xc = to_chunks(front_pad(xdt, pad), M2_CHUNK)
    ac = to_chunks(front_pad(da, pad), M2_CHUNK)
    bc = to_chunks(front_pad(b_in, pad), M2_CHUNK)
    cc = to_chunks(front_pad(c_in, pad), M2_CHUNK)
    a_cum = jnp.cumsum(ac, axis=2)
    causal = jnp.tril(jnp.ones((M2_CHUNK, M2_CHUNK), dtype=bool))
    seg = a_cum[:, :, :, None] - a_cum[:, :, None, :]
    l_mat = jnp.exp(jnp.where(causal[:, :, None, None], seg, -jnp.inf))
    cb = jnp.einsum('bnigs,bnjgs->bnijg', cc, bc)
    y_diag = jnp.einsum('bnijgh,bnjghp->bnighp', cb[..., None] * l_mat, xc)
    decay_to_end = jnp.exp(a_cum[:, :, -1:] - a_cum)
    u = jnp.einsum('bnjgs,bnjghp->bnghps', bc, xc * decay_to_end[..., None])
    chunk_decay = jnp.exp(a_cum[:, :, -1])

    def step(state, inp):
        c_n, e_n, u_n, d_n = inp
        y_n = jnp.einsum('bigs,bghps->bighp', c_n, state) * e_n[..., None]
        state = d_n[..., None, None] * state + u_n
        return state, y_n

    s0 = jnp.zeros((bsz, M2_GROUPS, M2_HPG, M2_HEADDIM, M2_STATE), f32)
    xs = (jnp.moveaxis(cc, 1, 0), jnp.moveaxis(jnp.exp(a_cum), 1, 0),
          jnp.moveaxis(u, 1, 0), jnp.moveaxis(chunk_decay, 1, 0))
    _, y_off = lax.scan(step, s0, xs)
    y = y_diag + jnp.moveaxis(y_off, 0, 1)
    y = y.reshape(bsz, lp, M2_GROUPS, M2_HPG, M2_HEADDIM)[:, pad:]
    y = y + d_skip.astype(f32).reshape(M2_GROUPS, M2_HPG, 1) * x_in
    y = y.reshape(bsz, length, M2_WIDTH) * jax.nn.silu(z.astype(f32))
    yg = y.reshape(bsz, length, M2_GROUPS, M2_WIDTH // M2_GROUPS)
    yg = yg * lax.rsqrt(jnp.mean(yg * yg, axis=-1, keepdims=True) + EPS)
    y = yg.reshape(bsz, length, M2_WIDTH) * norm_w.astype(f32)
    return y.astype(z.dtype)

def conv_glu_ffn(h, w_up, conv_w, conv_b, w_down):
    u = causal_dwconv_2(h @ w_up, conv_w, conv_b)
    gate, val = jnp.split(u, 2, axis=-1)
    return (jax.nn.silu(gate) * val) @ w_down

def second_inputs(seed: int = 0) -> dict:
    key = jax.random.key(seed)
    ks = jax.random.split(key, 20)
    f32 = jnp.float32

    def nrm(k, shape, scale):
        return scale * jax.random.normal(k, shape, f32)

    def gain(k, shape):
        return 1.0 + 0.05 * jax.random.normal(k, shape, f32)

    dt0 = jnp.exp(jax.random.uniform(ks[8], (DEPTH, M2_HEADS), f32,
                                     minval=math.log(DT_MIN), maxval=math.log(DT_MAX)))
    dt_bias = dt0 + jnp.log(-jnp.expm1(-dt0))
    a_log = jnp.log(jax.random.uniform(ks[9], (DEPTH, M2_HEADS), f32, minval=1.0, maxval=16.0))
    return {
        'x': nrm(ks[0], (BATCH, SEQ, D_MODEL), 1.0),
        'meta_tokens': nrm(ks[1], (N_META, D_MODEL), 1.0),
        'norm1_w': gain(ks[2], (DEPTH, D_MODEL)),
        'w_in': nrm(ks[3], (DEPTH, D_MODEL, D_PROJ), D_MODEL ** -0.5),
        'hg_lb_logits': nrm(ks[4], (DEPTH + 1, HG_KEY), 0.1),
        'hg_norm_w': gain(ks[5], (DEPTH, HG_WIDTH)),
        'm2_conv_w': nrm(ks[6], (DEPTH, M2_CONV, M2_XBC), M2_CONV ** -0.5),
        'm2_conv_b': nrm(ks[7], (DEPTH, M2_XBC), 0.02),
        'm2_dt_bias': dt_bias,
        'm2_a_log': a_log,
        'm2_d': gain(ks[10], (DEPTH, M2_HEADS)),
        'm2_norm_w': gain(ks[11], (DEPTH, M2_WIDTH)),
        'w_out': nrm(ks[12], (DEPTH, D_MIX, D_MODEL), D_MIX ** -0.5),
        'norm2_w': gain(ks[13], (DEPTH, D_MODEL)),
        'ffn_w_up': nrm(ks[14], (DEPTH, D_MODEL, 2 * D_FF), D_MODEL ** -0.5),
        'ffn_conv_w': nrm(ks[15], (DEPTH, FFN_CONV, 2 * D_FF), FFN_CONV ** -0.5),
        'ffn_conv_b': nrm(ks[16], (DEPTH, 2 * D_FF), 0.02),
        'ffn_w_down': nrm(ks[17], (DEPTH, D_FF, D_MODEL), D_FF ** -0.5),
        'final_norm_w': gain(ks[18], (D_MODEL,)),
    }

def second_block(x, meta_tokens, norm1_w, w_in, hg_lb_logits, hg_norm_w, m2_conv_w, m2_conv_b,
              m2_dt_bias, m2_a_log, m2_d, m2_norm_w, w_out, norm2_w, ffn_w_up, ffn_conv_w,
              ffn_conv_b, ffn_w_down, final_norm_w):
    bsz = x.shape[0]
    meta = jnp.broadcast_to(meta_tokens.astype(x.dtype)[None], (bsz, N_META, D_MODEL))
    h = jnp.concatenate([meta, x], axis=1)
    lbs = jnp.cumsum(jax.nn.softmax(hg_lb_logits.astype(jnp.float32), axis=0), axis=0)
    for l in range(DEPTH):
        u = rmsnorm_2(h, norm1_w[l])
        proj = u @ w_in[l]
        hg_q, hg_f, hg_i, hg_g, m2_z, m2_xbc, m2_dt = jnp.split(proj, PROJ_SPLITS, axis=-1)
        out_a = hgrn2_mixer(hg_q, hg_f, hg_i, hg_g, lbs[l], hg_norm_w[l])
        out_b = mamba2_mixer(m2_z, m2_xbc, m2_dt, m2_conv_w[l], m2_conv_b[l], m2_dt_bias[l],
                             m2_a_log[l], m2_d[l], m2_norm_w[l])
        h = h + jnp.concatenate([out_a, out_b], axis=-1) @ w_out[l]
        h = h + conv_glu_ffn(rmsnorm_2(h, norm2_w[l]), ffn_w_up[l], ffn_conv_w[l],
                             ffn_conv_b[l], ffn_w_down[l])
    y = rmsnorm_2(h, final_norm_w)
    return y[:, N_META:, :]


def setup_inputs(seed=0):
    out = dict(first_inputs(seed))
    for name, value in second_inputs(seed + 1).items():
        if name != "x":
            out[name + "_2"] = value
    return out


def reference(
    x, g_mix, w_in, gla_w_alpha, gla_b_alpha, gla_norm_g, conv_w, swa_sinks, w_gla_o, w_conv_o,
    w_swa_o, w_o, g_ffn, w_up, ffn_conv_w, w_down, g_final, meta_tokens_2, norm1_w_2, w_in_2,
    hg_lb_logits_2, hg_norm_w_2, m2_conv_w_2, m2_conv_b_2, m2_dt_bias_2, m2_a_log_2, m2_d_2,
    m2_norm_w_2, w_out_2, norm2_w_2, ffn_w_up_2, ffn_conv_w_2, ffn_conv_b_2, ffn_w_down_2,
    final_norm_w_2,
):
    x = first_block(
        x, g_mix, w_in, gla_w_alpha, gla_b_alpha, gla_norm_g, conv_w, swa_sinks, w_gla_o,
        w_conv_o, w_swa_o, w_o, g_ffn, w_up, ffn_conv_w, w_down, g_final,
    )
    return second_block(
        x, meta_tokens_2, norm1_w_2, w_in_2, hg_lb_logits_2, hg_norm_w_2, m2_conv_w_2,
        m2_conv_b_2, m2_dt_bias_2, m2_a_log_2, m2_d_2, m2_norm_w_2, w_out_2, norm2_w_2,
        ffn_w_up_2, ffn_conv_w_2, ffn_conv_b_2, ffn_w_down_2, final_norm_w_2,
    )


_drawn_inputs = setup_inputs


def setup_inputs(seed=0):
    import zlib

    import numpy as np

    out = dict(_drawn_inputs(seed))
    spreads = {}
    factors = {'gla_b_alpha': 8.0,
     'gla_norm_g': 7.108,
     'swa_sinks': 8.0,
     'g_ffn': 3.373,
     'hg_lb_logits_2': 8.0,
     'hg_norm_w_2': 3.248,
     'm2_conv_b_2': 3.42,
     'm2_d_2': 2.761,
     'ffn_conv_b_2': 4.798}
    for name, (base, spread) in spreads.items():
        noise = np.random.default_rng([zlib.crc32(name.encode()), seed]).standard_normal(out[name].shape)
        drawn = base * np.exp(spread * noise) if base else spread * noise
        out[name] = jnp.asarray(drawn.astype(out[name].dtype))
    for name, factor in factors.items():
        out[name] = (out[name] * factor).astype(out[name].dtype)
    return out
```

```python
from contextlib import ExitStack

import numpy as np

import concourse.bass as bass
from concourse import mybir

ALU = mybir.AluOpType
ACT = mybir.ActivationFunctionType
AXX = mybir.AxisListType.X
F32 = mybir.dt.float32
F32R = mybir.dt.float32r
I32 = mybir.dt.int32

P = 128
D = 1024
KD = D // P
SEQ = 512
META = 16
T2 = META + SEQ
BLK = 128
NBLK = SEQ // BLK
BANK = 512
EPS = 1e-6
GLA_H, GLA_C, GLA_RANK, GLA_TAU = 4, 64, 16, 16.0
SWA_G, SWA_T, SWA_HD, SWA_W = 2, 4, 64, 128
CONV_T = 4
FF = 2816
FT = FF // P
HG_H, HG_C = 8, 16
M2_T, M2_H, M2_G, M2_P = 8, 16, 2, 64
SUB = BLK // HG_C
USED = META - 4

UNIT = 128
PER = 8
RAW = 3
SPL = 3
AHEAD = SPL - 1


def plan():
    groups = []

    def full(kind, n, matrix, col, op="u", k=KD, k0=0):
        groups.append((kind, n, [(matrix, k0 + i, col, op, i) for i in range(k)]))

    o, at = {}, 0
    for name, n in (("gq", 512), ("gk", 512), ("gv", 512), ("gr", 512), ("ga", 16), ("cx", 512), ("cb", 512),
                    ("cc", 512), ("sq", 512), ("sk", 128), ("sv", 128), ("gates", 3072)):
        o[name] = at
        at += n
    full("ga", 0, "w_in", o["ga"])
    for h in range(GLA_H):
        for name in ("gq", "gk", "gv", "gr"):
            full(name, h, "w_in", o[name] + h * P)
    full("sk", 0, "w_in", o["sk"])
    full("sv", 0, "w_in", o["sv"])
    for t in range(SWA_T):
        full("sq", t, "w_in", (o["sq"] + t * SWA_HD, o["sq"] + (t + SWA_T) * SWA_HD))
    for t in range(CONV_T):
        for name in ("cc", "cx", "cb"):
            full(name, t, "w_in", o[name] + t * P)
    for m in range(KD):
        for br, matrix in enumerate(("w_gla_o", "w_conv_o", "w_swa_o")):
            full("gate", (m, br), "w_in", o["gates"] + br * D + m * P)
            full("y", (m, br), matrix, m * P, "y%d" % br, 4)
    for m in range(KD):
        full("wo", m, "w_o", m * P, "m")
    for j in range(FT):
        full("up", (j, 0), "w_up", j * P)
        full("up", (j, 1), "w_up", FF + j * P)
    for m in range(KD):
        full("down", m, "w_down", m * P, "a", FT)
    first2 = len(groups)
    hq, hf, hi, hg, mz, mx, mb, mc, dt = 0, 1024, 2048, 3072, 4096, 5120, 6144, 6400, 6656
    for h in range(HG_H):
        full("hf", h, "w_in_2", hf + h * P)
        full("hq", h, "w_in_2", hq + h * P)
        full("hi", h, "w_in_2", hi + h * P)
        full("hg", h, "w_in_2", hg + h * P)
    full("dt", 0, "w_in_2", dt)
    for g in range(M2_G):
        full("mb", g, "w_in_2", mb + g * P)
    for g in range(M2_G):
        full("mc", g, "w_in_2", mc + g * P)
    for t in range(M2_T):
        full("mx", t, "w_in_2", mx + t * P)
        full("oh", t, "w_out_2", t * P, "v")
    for t in range(M2_T):
        full("mz", t, "w_in_2", mz + t * P)
    for m in range(KD):
        full("om", m, "w_out_2", m * P, "v", KD, KD)
    for j in range(FT):
        full("up2", (j, 0), "ffn_w_up_2", j * P)
        full("up2", (j, 1), "ffn_w_up_2", FF + j * P)
    for m in range(KD):
        full("down2", m, "ffn_w_down_2", m * P, "a", FT)
    return groups, first2


GROUPS, FIRST2 = plan()
NG = len(GROUPS)
FIRST_UNIT = [0]
for _g in GROUPS:
    FIRST_UNIT.append(FIRST_UNIT[-1] + len(_g[2]))
UNITS = [u for g in GROUPS for u in g[2]]
SLABS = -(-len(UNITS) // PER)
GROUP_OF = {(k, i): n for n, (k, i, _) in enumerate(GROUPS)}
ENDS = sorted({FIRST_UNIT[g + 1] - 1 for g in range(NG)}
              | {min(PER * (s + 1), len(UNITS)) - 1 for s in range(SLABS)})
END_NO = {u: n + 1 for n, u in enumerate(ENDS)}


def group_end(g):
    return END_NO[FIRST_UNIT[g + 1] - 1]


def slab_end(s):
    return END_NO[min(PER * (s + 1), len(UNITS)) - 1]


SLOTS1, SLOTS2 = 3, 2


def slot_of(g):
    return g % SLOTS1 if g < FIRST2 else SLOTS1 + (g - FIRST2) % SLOTS2


TURN = []
_used = [0] * (SLOTS1 + SLOTS2)
for _n in range(NG):
    TURN.append(_used[slot_of(_n)])
    _used[slot_of(_n)] += 1
LAST1 = [max(n for n in range(FIRST2) if slot_of(n) == s) for s in range(SLOTS1)]


def columns(g):
    kind = GROUPS[g][0]
    if g < FIRST2 or kind == "down2":
        return META, T2
    return (USED, T2) if kind in ("oh", "om", "up2") else (0, T2)


def base_of(g):
    n = columns(g)[1] - columns(g)[0]
    if g < FIRST2:
        return slot_of(g) * BANK
    first = 2 * BANK * (slot_of(g) - SLOTS1)
    return first if n <= BANK else first + BANK - n // 2


def halves(n):
    return [(0, n)] if n <= BANK else [(0, n // 2), (n // 2, n)]


SSM_SUM = 6 * BANK - T2 // 2

PCOL, NPAR = {}, 0
for _name, _n in (("g_mix", 8), ("g_ffn", 8), ("b_alpha", 4), ("gla_norm", 4), ("conv", 12), ("sinks", 8),
                  ("fconv", 6 * FT), ("norm1", 8), ("lb0", 8), ("lb1", 8), ("hg_norm", 8), ("m2conv", 48),
                  ("m2convb", 12), ("dt_bias", 1), ("a_log", 1), ("m2d", 8), ("m2norm", 8), ("norm2", 8), ("g_final", 8),
                  ("fconv2", 6 * FT), ("fconvb2", 2 * FT), ("final", 8), ("eps", 1)):
    PCOL[_name] = NPAR
    NPAR += _n


def schedule():
    after = {g: [] for g in range(NG)}

    def put(kind, idx, *what):
        after[GROUP_OF[(kind, idx)]].extend(what)

    for n, names, heads, tail in (
        (0, ("gq", "gk", "gv", "gr"), GLA_H, (("sk", 0), ("sv", 0), ("sq", 0), ("sq", 1))),
        (GLA_H, ("hf", "hq", "hi", "hg"), HG_H, (("dt", 0), ("mb", 0), ("mb", 1), ("mc", 0))),
    ):
        for h in range(heads):
            at = [(k, h + 1) for k in names] if h + 1 < heads else tail
            put(names[3], h, ("prep", n + h))
            nxt = [(k, h + 2) for k in names] if h + 2 < heads else tail if h + 2 == heads else (
                ("sq", 2) if n == 0 else ("mc", 1),)
            if h + 1 < heads:
                at = [at[1], at[2], at[3], nxt[0]]
            else:
                at = list(at[1:4]) + [nxt[0]]
            for stage, where in zip("abcd", at):
                put(*where, ("head_" + stage, n + h))
    for g in after:
        after[g].sort(key=lambda s: s[0] == "prep")
    put("sq", 3, ("swa_v", 0))
    fill = [(n, t) for t in range(CONV_T) for n in ("cc", "cx", "cb")]
    stages = [(s, 2 * b + g) for b in range(NBLK) for g in range(SWA_G) for s in ("swa_a", "swa_b", "swa_c")]
    for n, st in enumerate(stages):
        put(*fill[min(n // 2, len(fill) - 1)], st)
    for kind, which in (("wo", "g_ffn"), ("down", "norm1"), ("om", "norm2"), ("down2", "final")):
        for k in range(KD):
            put(kind, k, ("square", (which, k)))
        put(kind, KD - 1, ("norm", which))
    put("down", KD - 1, ("bounds", 0))
    put("hf", 0, ("second_start", 0))
    put("hq", 0, ("second_start", 1))
    put("mx", 0, ("ssm_dt", 0), ("ssm_bc", 0))

    put("oh", 0, ("ssm_bc", 1))
    for t in range(M2_T):
        put("oh", t, ("ssm_a", t))
        if t + 1 < M2_T:
            put("mx", t + 1, ("ssm_b", t))
            after[GROUP_OF[("oh", t + 1)]].insert(0, ("ssm_c", t))
        else:
            put("mz", 0, ("ssm_b", t))
            put("mz", 1, ("ssm_c", t))
    for t in range(M2_T):
        put("mz", min(t + 1, M2_T - 1), ("ssm_sum", t))
        if t % 4 == 3:
            put("mz", min(t + 1, M2_T - 1), ("ssm_norm", t // 4))
    steps = [("square", ("g_mix", k)) for k in range(KD)] + [("norm", "g_mix")]
    for g in range(NG):
        steps.append(("group", g))
        steps.extend(after[g])
    return steps


STEPS = schedule()
NORMS = ["g_mix", "g_ffn", "norm1", "norm2", "final"]


TILE_NO = {}
for _kind, _i in STEPS:
    _new = []
    if _kind == "head_d":
        _new = [("y", _i) if _i < GLA_H else ("v", _i - GLA_H)]
    if _kind == "ssm_norm":
        _new = [("v2", 4 * _i + t) for t in range(4)]
    if _kind == "group":
        _k, _j, _ = GROUPS[_i]
        _new = {"cb": [("y", GLA_H + (_j if _k == "cb" else 0))], "y": [("m", _j[0])] if _k == "y" and _j[1] == 2 else [],
                "up": [("a", _j[0])] if _k == "up" and _j[1] else [],
                "up2": [("a2", _j[0])] if _k == "up2" and _j[1] else []}.get(_k, [])
    for _t in _new:
        TILE_NO[_t] = len(TILE_NO) + 1


BOTH = ("gr", "hg", "hf", "hq", "up", "up2", "mx", "mb", "mc", "mz")
PART_NO = {g: n + 1 for n, g in enumerate(g for g in range(NG) if GROUPS[g][0] in BOTH)}


def m2_channel(kind, i):
    return i + {"mx": 0, "mb": M2_T, "mc": M2_T + M2_G}[kind]


def norm_columns(which):
    return {"norm2": (USED, T2)}.get(which, (META, T2))


def program(nc, weights, xT, metaT, params, consts, cmask, w_alpha, outT):
    with ExitStack() as ctx:
        def sb(name, shape, dt=F32, scope=ctx):
            return scope.enter_context(nc.sbuf_tensor(name, shape, dt))

        def sem(name):
            return ctx.enter_context(nc.semaphore(name))

        ps = ctx.enter_context(nc.psum_tensor("ps", [P, 8, BANK], F32))
        pf = ps[:].rearrange("p b n -> p (b n)")

        h_res = sb("h_res", [P, KD, T2])
        u_hi = sb("u_hi", [P, KD, T2], F32R)
        u_lo = sb("u_lo", [P, KD, T2], F32R)
        w_raw = sb("w_raw", [P, RAW, PER * UNIT])
        w_hi = sb("w_hi", [P, SPL, PER * UNIT], F32R)
        w_lo = sb("w_lo", [P, SPL, PER * UNIT], F32R)
        par = sb("par", [P, NPAR])
        cst = sb("cst", [P, 416 + 2 * T2 + SEQ])
        ones = sb("ones", [P, P])
        msk = sb("msk", [P, P], I32)
        r_bc = sb("r_bc", [P, T2])
        gain1 = sb("gain1", [P, KD])
        full = sb("full", [P, 2, T2])
        ident = cst[:, 0:128]
        dist = cst[:, 128:384]
        first8 = cst[:, 384:416]
        seg16 = cst[:, 416:416 + T2]
        seg128 = cst[:, 416 + T2:416 + 2 * T2]
        seg64 = cst[:, 416 + 2 * T2:416 + 2 * T2 + SEQ]

        def pc(name, i=0, rows=P):
            return par[0:rows, PCOL[name] + i:PCOL[name] + i + 1]

        def carve(arena):
            at = [0]

            def take(*shape, at_=None):
                n = int(np.prod(shape))
                a = at[0] if at_ is None else at_
                at[0] = max(at[0], a + n)
                v = arena[:, a:a + n]
                if len(shape) == 2:
                    v = v.rearrange("p (a b) -> p a b", b=shape[1])
                if len(shape) == 3:
                    v = v.rearrange("p (a b c) -> p a b c", b=shape[1], c=shape[2])
                return v
            return take, at

        s1 = ExitStack()
        y_hi = sb("y_hi", [P, 12, SEQ], F32R, s1)
        y_lo = sb("y_lo", [P, 12, SEQ], F32R, s1)
        s1a = ExitStack()
        arena1 = sb("arena1", [P, 27 * SEQ + 64], F32, s1a)
        s1a.close()
        m_hi = sb("m_hi", [P, KD, SEQ], F32R, s1)
        m_lo = sb("m_lo", [P, KD, SEQ], F32R, s1)
        mrg = sb("mrg", [P, 5, SEQ], F32, s1)
        s1.close()
        s2 = ExitStack()
        a_hi = sb("a_hi", [P, FT, SEQ], F32R, s2)
        a_lo = sb("a_lo", [P, FT, SEQ], F32R, s2)
        ffn = sb("ffn", [P, 7, SEQ], F32, s2)
        s2.close()
        s3 = ExitStack()
        v_hi = sb("v_hi", [P, KD, T2], F32R, s3)
        v_lo = sb("v_lo", [P, KD, T2], F32R, s3)
        N3 = 18144
        arena2 = sb("arena2", [P, N3], F32, s3)
        s3.close()

        take, at = carve(arena1[:, :])
        ge = take(4, SEQ)
        gt1, gt2, gcum = take(SEQ), take(SEQ), take(SEQ)
        g_qE, g_kE = take(SEQ), take(SEQ)
        g_kZ, g_qZ = take(NBLK, BLK), take(NBLK, BLK)
        g_kL, g_qB = take(NBLK, 64), take(NBLK, 64)
        qf1, kf1, vf1 = take(SEQ), take(SEQ), take(SEQ)
        g_attn, g_ktok, g_vtok, g_state = (take(NBLK, BLK) for _ in range(4))
        g_o, g_osq, g_or = take(SEQ), take(SEQ), take(SEQ)
        g_gate = take(2, SEQ)
        ga_sb, wal = take(SEQ), take(GLA_H * P)
        g_D, negb = take(NBLK), take(GLA_H)
        off = {"ge": 0, "gt1": 4 * SEQ, "gt2": 5 * SEQ, "gcum": 6 * SEQ, "qE": 7 * SEQ, "kZ": 9 * SEQ,
               "kL": 11 * SEQ, "qf": 12 * SEQ, "kf": 13 * SEQ, "attn": 15 * SEQ, "o": 19 * SEQ}
        s_q = take(SWA_T, SEQ, at_=off["ge"])
        s_k, s_vf = take(SEQ, at_=off["gt1"]), take(SEQ, at_=off["gt2"])
        s_vtok = take(NBLK, P, at_=off["gcum"])
        s_L = take(SWA_T, 256, at_=off["qE"])
        s_P = take(SWA_T, 256, at_=off["kZ"])
        s_PT = take(SWA_T, 2, BLK, at_=off["attn"])
        s_small = take(8, SWA_T, at_=off["kL"])
        c_c = take(SEQ, at_=off["qf"])
        c_u = take(SEQ + 2, at_=off["kf"])
        c_y, c_a = take(SEQ, at_=off["o"]), take(SEQ, at_=off["o"] + SEQ)

        take, at = carve(arena2[:, :])
        fs, k2, qs0 = take(T2), take(T2), take(T2)
        t21, t22, lf2, bc2 = take(T2), take(T2), take(T2), take(T2)
        e2 = take(4, T2)
        vf2 = take(T2)
        KC = take(NBLK, (SUB + 1) * BLK)
        kcm = take(2, META)
        qd2, qz2 = take(T2), take(NBLK, BLK)
        h_attn, h_ktok, h_vtok, h_state = (take(NBLK, BLK) for _ in range(4))
        h_am, h_ktm, h_vtm = take(META), take(P), take(P)
        h_o, h_osq, h_or = take(T2), take(T2), take(T2)
        h_gate = take(2, T2)
        dshift, dcum, h_D = take(32), take(32), take(NBLK)
        lb, lb1 = take(HG_H), take(HG_H)
        fs1, qs1 = take(T2), take(T2)
        f2, q2 = (fs, fs1), (qs0, qs1)
        hg_end = at[0]
        m_bc = take(4, T2, at_=0)
        dt_t, ac_t, sp1, sp2 = (take(T2, at_=(4 + i) * T2) for i in range(4))
        cv = take(2, T2, at_=8 * T2)
        m_cols = take(2, NBLK, M2_H, at_=10 * T2)
        m_colm = take(2, M2_H, at_=10 * T2 + 2 * NBLK * M2_H)
        m_a = take(1, at_=10 * T2 + 2 * NBLK * M2_H + 2 * M2_H)
        m_al = take(2, NBLK, at_=10 * T2 + 2 * NBLK * M2_H + 2 * M2_H + 8)
        m_dte = take(2, NBLK, at_=10 * T2 + 2 * NBLK * M2_H + 2 * M2_H + 24)
        m_dec = take(2, NBLK, at_=10 * T2 + 2 * NBLK * M2_H + 2 * M2_H + 32)
        m_dtm = take(2, at_=10 * T2 + 2 * NBLK * M2_H + 2 * M2_H + 40)
        o2 = 12 * T2
        m_y = take(M2_T, T2, at_=o2)
        o2 += M2_T * T2
        m_bt = take(2, NBLK, P, at_=o2)
        m_btm = take(2, P, at_=o2 + 8 * P)
        m_cb = take(2, NBLK, BLK, at_=o2 + 10 * P)
        m_cbm = take(2, META, at_=o2 + 18 * P)
        o2 += 18 * P + 2 * META
        m_x = take(2, T2, at_=o2)
        o2 += 2 * T2
        m_er = take(2, T2, at_=o2)
        o2 += 2 * T2
        m_at = take(2, NBLK, BLK, at_=o2)
        m_atm = take(2, META, at_=o2 + 8 * BLK)
        o2 += 8 * BLK + 2 * META
        m_xt = take(3, NBLK, P, at_=o2)
        m_xtm = take(3, P, at_=o2 + 12 * P)
        o2 += 15 * P
        m_st = take(NBLK, P, at_=11 * T2)
        assert max(o2, hg_end) <= N3, (o2, hg_end, N3)

        par_in, meta_in, alpha_in = sem("par_in"), sem("meta_in"), sem("alpha_in")
        x_in = [sem(f"x_in{i}") for i in range(KD // 2)]
        w_in = [sem(f"w_in{i}") for i in range(RAW)]
        w_hi_ok, w_lo_ok, unit_end = sem("w_hi_ok"), sem("w_lo_ok"), sem("unit_end")
        acc_free = [sem(f"acc_free{i}") for i in range(SLOTS1 + SLOTS2)]
        dve_chain, act_chain, zeroed = sem("dve_chain"), sem("act_chain"), sem("zeroed")
        sq_ok, sq_added, sum_ok, rstd_ok = sem("sq_ok"), sem("sq_added"), sem("sum_ok"), sem("rstd_ok")
        sq2_ok, sq2_added, meta_sq, meta_sum = sem("sq2_ok"), sem("sq2_added"), sem("meta_sq"), sem("meta_sum")
        first_rstd, scaled_sum = sem("first_rstd"), sem("scaled_sum")
        u_full, u_hi_ok, u_lo_ok = sem("u_full"), sem("u_hi_ok"), sem("u_lo_ok")
        out_ok, out_done = sem("out_ok"), sem("out_done")
        tile_lo = sem("tile_lo")
        act_part, silu_ok, f_ok = sem("act_part"), sem("silu_ok"), sem("f_ok")
        negb_ok, lbd_ok, lbe_ok, lb_ok = sem("negb_ok"), sem("lbd_ok"), sem("lbe_ok"), sem("lb_ok")
        pa_ok, sp_ok, cum_ok, exp_ok, ready = (sem(x) for x in ("pa_ok", "sp_ok", "cum_ok", "exp_ok", "ready"))
        st_a, st_b, st_c, st_d = sem("st_a"), sem("st_b"), sem("st_c"), sem("st_d")
        attn_ok, tok_ok, state_ok, o_ok, r_ok = (sem(x) for x in ("attn_ok", "tok_ok", "state_ok", "o_ok", "r_ok"))
        sw_s, sw_m, sw_e, sw_p, sw_t, sw_pt, sw_o = (sem(f"swa_{x}") for x in
                                                     ("scores", "max", "exp", "prob", "turned", "probT", "out"))
        sv_t, sv_ok, sw_hi, sw_lo = sem("sv_turned"), sem("sv_ok"), sem("swa_hi"), sem("swa_lo")
        ssm_sem = {x: sem("ssm_" + x) for x in
                   ("a0", "dt", "cum", "turned", "cols", "bct", "bt", "cb", "x", "A", "row", "diff", "exp", "alast",
                    "dte", "xt", "attn", "ce", "B", "state", "C", "y", "sq", "sum", "r", "n")}
        block = ctx.enter_context(nc.Block())

        def acc(g, rows=P):
            c0, c1 = columns(g)
            return pf[0:rows, base_of(g):base_of(g) + c1 - c0]

        def product_done(eng, g):
            eng.wait_ge(unit_end, group_end(g))

        def evacuated(eng, g):
            eng.wait_ge(acc_free[slot_of(g)], TURN[g] + 1)

        def sums(which):
            c0, c1 = norm_columns(which)
            first = 7 * BANK if c1 - c0 <= BANK else 7 * BANK - (c1 - c0) // 2
            return first, c1 - c0

        def residual_ready(eng, which, k):
            if which == "g_mix":
                eng.wait_ge(x_in[k // 2], 16)
            else:
                evacuated(eng, GROUP_OF[({"g_ffn": "wo", "norm1": "down", "norm2": "om", "final": "down2"}[which], k)])

        def main(v):
            return v[:, META:T2].rearrange("p (b t) -> p b t", t=BLK)

        @block.sync
        def _(sp):
            x_v = xT.rearrange("(k p) t -> p k t", p=P)
            for k in range(0, KD, 2):
                sp.dma_start(h_res[:, k:k + 2, META:T2], x_v[:, k:k + 2, :]).then_inc(x_in[k // 2], 16)
            sp.dma_start(par[:, :], params).then_inc(par_in, 16)
            for s in range(SLABS):
                if s >= RAW:
                    sp.wait_ge(w_lo_ok, s - RAW + 1)
                n = min(PER, len(UNITS) - PER * s) * UNIT
                sp.dma_start(w_raw[:, s % RAW, 0:n], weights[s, :, 0:n]).then_inc(w_in[s % RAW], 16)
                if s == 0:
                    sp.dma_start(cst[:, :], consts).then_inc(par_in, 16)
                    sp.dma_start(msk[:, :], cmask).then_inc(par_in, 16)
                    sp.dma_start(wal[0:GLA_RANK, :], w_alpha).then_inc(alpha_in, 16)
                    sp.dma_start(h_res[:, :, 0:META], metaT.rearrange("(k p) t -> p k t", p=P)).then_inc(meta_in, 16)
            out_v = outT.rearrange("(k p) t -> p k t", p=P)
            for k in range(KD):
                sp.wait_ge(out_ok, k + 1)
                sp.dma_start(out_v[:, k, :], h_res[:, k, META:T2]).then_inc(out_done, 16)
            sp.wait_ge(out_done, 16 * KD)

        @block.gpsimd
        def _(pool):
            for s in range(SLABS):
                n = min(PER, len(UNITS) - PER * s) * UNIT
                pool.wait_ge(w_hi_ok, s + 1)
                nc.gpsimd.tensor_tensor(w_lo[:, s % SPL, 0:n], w_raw[:, s % RAW, 0:n], w_hi[:, s % SPL, 0:n],
                                        ALU.subtract).then_inc(w_lo_ok, 1)

        @block.tensor
        def _(pe):
            def mm(out, lhsT, rhs, start=True, stop=True):
                return nc.tensor.matmul(out, lhsT, rhs, start=start, stop=stop)

            def turn(out, x):
                k = x.shape[0]
                return nc.tensor.transpose(out, x, ident[0:k, 0:k])

            def group(g):
                kind, idx, units = GROUPS[g]
                c0, c1 = columns(g)
                if TURN[g]:
                    evacuated(pe, [k for k in range(g) if slot_of(k) == slot_of(g)][-1])
                elif g >= FIRST2:
                    for k in LAST1:
                        evacuated(pe, k)
                rows = {"ga": GLA_RANK, "dt": M2_H}.get(kind, P)
                out = acc(g, rows)
                for n, (_, _, _, op, i) in enumerate(units):
                    u = FIRST_UNIT[g] + n
                    s, w = u // PER, UNIT * (u % PER)
                    if n == 0 or u % PER == 0:
                        pe.wait_ge(w_lo_ok, s + 1)
                    if op == "u":
                        hi, lo = u_hi[:, i, c0:c1], u_lo[:, i, c0:c1]
                        which = "g_mix" if g < GROUP_OF[("up", (0, 0))] else "g_ffn" if g < FIRST2 else (
                            "norm2" if kind == "up2" else "norm1")
                        pe.wait_ge(u_lo_ok, KD * NORMS.index(which) + i + 1)
                    elif op[0] == "y":
                        hi, lo = y_hi[:, 4 * int(op[1]) + i, :], y_lo[:, 4 * int(op[1]) + i, :]
                        if op == "y2":
                            pe.wait_ge(sw_lo, SWA_G * NBLK)
                        else:
                            pe.wait_ge(tile_lo, TILE_NO[("y", 4 * int(op[1]) + i)])
                    elif op == "m":
                        hi, lo = m_hi[:, i, :], m_lo[:, i, :]
                        pe.wait_ge(tile_lo, TILE_NO[("m", i)])
                    elif op == "a":
                        hi, lo = a_hi[:, i, :], a_lo[:, i, :]
                        pe.wait_ge(tile_lo, TILE_NO[("a" if kind == "down" else "a2", i)])
                    else:
                        hi, lo = v_hi[:, i, c0:c1], v_lo[:, i, c0:c1]
                        pe.wait_ge(tile_lo, TILE_NO[("v" if kind == "oh" else "v2", i)])
                    wh, wl = w_hi[:, s % SPL, w:w + rows], w_lo[:, s % SPL, w:w + rows]
                    cuts = halves(c1 - c0)
                    for j, (wt, x) in enumerate(((wh, hi), (wl, hi), (wh, lo))):
                        for a, b in cuts:
                            last = mm(out[:, a:b], wt, x[:, a:b], start=(n == 0 and j == 0),
                                      stop=(n == len(units) - 1 and j == 2))
                    if u in END_NO:
                        last.then_inc(unit_end, 1)

            def norm(which):
                first, n = sums(which)
                pe.wait_ge(zeroed, 1)
                pe.wait_ge(sq_added, (KD - 1) * (NORMS.index(which) + 1))
                for a, b in halves(n):
                    last = mm(pf[:, first + a:first + b], ones[:, :], r_bc[:, a:b])
                if which == "norm1":
                    pe.wait_ge(meta_sum, 1)
                    mm(ps[:, 5, 0:META], ones[:, :], ffn[:, 4, 0:META])
                    pe.wait_ge(sq2_added, KD - 1)
                    last = mm(ps[:, 6, :], ones[:, :], ffn[:, 0, :])
                last.then_inc(sum_ok, 1)

            def prep(n):
                if n < GLA_H:
                    if n == 0:
                        evacuated(pe, GROUP_OF[("ga", 0)])
                        pe.wait_ge(alpha_in, 16)
                    else:
                        pe.wait_ge(sp_ok, n)
                    mm(ps[:, 7, :], wal[0:GLA_RANK, n * P:(n + 1) * P], ga_sb[0:GLA_RANK, :]).then_inc(pa_ok, 1)

            def head_a(n):
                pe.wait_ge(ready, n + 1)
                gla = n < GLA_H
                evacuated(pe, GROUP_OF[("gv", n) if gla else ("hi", n - GLA_H)])
                if n:
                    pe.wait_ge(state_ok, n)
                    pe.wait_ge(o_ok, n)
                    pe.wait_ge(r_ok, n)
                if n == 0:
                    pe.wait_ge(par_in, 48)
                for b in range(NBLK):
                    at = b * BLK
                    if gla:
                        c = GLA_C
                        mm(ps[:, 4, at:at + c], g_kE[:, at:at + BLK], g_qE[:, at:at + c])
                        mm(ps[0:c, 4, at + c:at + BLK], g_kL[:, b, :], g_qB[:, b, :])
                        mm(ps[c:BLK, 4, at + c:at + BLK], g_kE[:, at + c:at + BLK], g_qE[:, at + c:at + BLK])
                        turn(ps[:, 5, at:at + BLK], g_kZ[:, b, :])
                        last = turn(ps[:, 6, at:at + BLK], vf1[:, at:at + BLK])
                    else:
                        for c in range(SUB):
                            q0 = META + at + HG_C * c
                            mm(ps[:, 4, at + HG_C * c:at + HG_C * (c + 1)], KC[:, b, c * BLK:(c + 1) * BLK],
                               qd2[:, q0:q0 + HG_C])
                        turn(ps[:, 5, at:at + BLK], KC[:, b, SUB * BLK:(SUB + 1) * BLK])
                        last = turn(ps[:, 6, at:at + BLK], vf2[:, META + at:META + at + BLK])
                if not gla:
                    mm(ps[0:META, 7, 0:16], kcm[:, 0, :], qd2[:, 0:META])
                    turn(ps[0:META, 7, 16:144], kcm[:, 1, :])
                    last = turn(ps[0:META, 7, 144:272], vf2[:, 0:META])
                last.then_inc(st_a, 1)

            def head_b(n):
                gla = n < GLA_H
                kt, vt = (g_ktok, g_vtok) if gla else (h_ktok, h_vtok)
                pe.wait_ge(tok_ok, n + 1)
                pe.wait_ge(attn_ok, n + 1)
                if not gla:
                    mm(ps[:, 7, 272:400], h_ktm[0:META, :], h_vtm[0:META, :])
                for b in range(NBLK - 1):
                    last = mm(ps[:, 4, b * BLK:(b + 1) * BLK], kt[:, b, :], vt[:, b, :])
                last.then_inc(st_b, 1)

            def head_c(n):
                gla = n < GLA_H
                vt, at_, st, qz = (g_vtok, g_attn, g_state, g_qZ) if gla else (h_vtok, h_attn, h_state, qz2)
                pe.wait_ge(state_ok, n + 1)
                for b in range(NBLK):
                    out = ps[:, 5, b * BLK:(b + 1) * BLK]
                    inter = not gla or b > 0
                    last = mm(out, vt[:, b, :], at_[:, b, :], stop=not inter)
                    if inter:
                        last = mm(out, st[:, b, :], qz[:, b, :], start=False)
                if not gla:
                    last = mm(ps[:, 7, 400:416], h_vtm[0:META, :], h_am[0:META, :])
                last.then_inc(st_c, 1)

            def head_d(n):
                gla = n < GLA_H
                pe.wait_ge(o_ok, n + 1)
                last = mm(ps[:, 6, :], ones[:, :], g_osq if gla else h_osq[:, META:T2])
                if not gla:
                    last = mm(ps[:, 7, 416:432], ones[:, :], h_osq[:, 0:META])
                last.then_inc(st_d, 1)

            def swa_v():
                evacuated(pe, GROUP_OF[("sv", 0)])
                for b in range(NBLK):
                    last = turn(ps[:, 4, b * P:(b + 1) * P], s_vf[:, b * P:(b + 1) * P])
                last.then_inc(sv_t, 1)

            def swa_a(n):
                b, g = n // SWA_G, n % SWA_G
                lo = slice(SWA_HD * g, SWA_HD * (g + 1))
                if n == 0:
                    evacuated(pe, GROUP_OF[("sk", 0)])
                    evacuated(pe, GROUP_OF[("sq", SWA_T - 1)])
                    pe.wait_ge(sv_ok, 1)
                else:
                    pe.wait_ge(sw_m, n)
                c0 = SWA_W if b == 0 else 0
                for t in range(SWA_T):
                    col = 4 * BANK + 256 * t
                    last = mm(pf[:, col + c0:col + 256], s_q[lo, t, b * BLK:(b + 1) * BLK],
                              s_k[lo, (b - 1) * BLK + c0:(b + 1) * BLK])
                last.then_inc(sw_s, 1)

            def swa_b(n):
                b = n // SWA_G
                pe.wait_ge(sw_p, n + 1)
                if n:
                    pe.wait_ge(sw_pt, n)
                for t in range(SWA_T):
                    for j in range(1 if b == 0 else 0, 2):
                        col = 6 * BANK + 256 * t + BLK * j
                        last = turn(pf[:, col:col + BLK], s_P[:, t, j * BLK:(j + 1) * BLK])
                last.then_inc(sw_t, 1)

            def swa_c(n):
                b, g = n // SWA_G, n % SWA_G
                lo = slice(SWA_HD * g, SWA_HD * (g + 1))
                pe.wait_ge(sw_pt, n + 1)
                if n:
                    pe.wait_ge(sw_lo, n)
                for t in range(SWA_T):
                    js = range(1 if b == 0 else 0, 2)
                    for j in js:
                        last = mm(ps[lo, 3, t * BLK:(t + 1) * BLK], s_vtok[:, b - 1 + j, lo], s_PT[:, t, j, :],
                                  start=(j == js[0]), stop=(j == 1))
                last.then_inc(sw_o, 1)

            S = ssm_sem

            def ssm_dt():
                pe.wait_ge(S["cum"], 1)
                pe.wait_ge(r_ok, GLA_H + HG_H)
                for i, v in enumerate((ac_t, dt_t)):
                    for b in range(NBLK):
                        turn(ps[:, 7, 64 * i + 16 * b:64 * i + 16 * b + 16],
                             v[0:M2_H, META + b * BLK:META + (b + 1) * BLK])
                    last = turn(ps[0:META, 7, 128 + 16 * i:144 + 16 * i], v[0:M2_H, 0:META])
                last.then_inc(S["turned"], 1)

            def ssm_bc(g):
                pe.wait_ge(S["x"], 2 * M2_G if g else 2 * M2_G)
                pe.wait_ge(S["cols"], 1)
                if g:
                    pe.wait_ge(S["bt"], g)
                    pe.wait_ge(S["cb"], g)
                for b in range(NBLK):
                    cols = slice(META + b * BLK, META + (b + 1) * BLK)
                    turn(ps[:, 4, b * P:(b + 1) * P], m_bc[:, g, cols])
                    mm(ps[:, 5, b * P:(b + 1) * P], m_bc[:, g, cols], m_bc[:, 2 + g, cols])
                turn(ps[0:META, 7, 0:128], m_bc[:, g, 0:META])
                mm(ps[0:META, 7, 128:144], m_bc[:, g, 0:META], m_bc[:, 2 + g, 0:META]).then_inc(S["bct"], 1)

            def ssm_a(t):
                pe.wait_ge(S["x"], 2 * M2_G + t + 1)
                if t == 0:
                    pe.wait_ge(S["bt"], M2_G)
                    pe.wait_ge(S["cb"], M2_G)
                else:
                    pe.wait_ge(S["y"], t)
                    pe.wait_ge(S["state"], t)
                for i in range(2):
                    pick = ident[0:M2_H, 2 * t + i:2 * t + i + 1].broadcast_to((M2_H, P))
                    mm(ps[:, 4 + i, :], pick, ac_t[0:M2_H, META:T2])
                    mm(ps[0:META, 7, 16 * i:16 * i + 16], pick[:, 0:META], ac_t[0:M2_H, 0:META])
                for b in range(NBLK):
                    turn(ps[:, 6, b * P:(b + 1) * P], m_x[:, t % 2, META + b * BLK:META + (b + 1) * BLK])
                turn(ps[0:META, 7, 32:160], m_x[:, t % 2, 0:META]).then_inc(S["A"], 1)

            def ssm_b(t):
                g = t // 4
                pe.wait_ge(S["xt"], t + 1)
                mm(ps[:, 7, 160:288], m_btm[0:META, g, :], m_xtm[0:META, 2, :])
                for b in range(NBLK - 1):
                    last = mm(ps[:, 6, b * P:(b + 1) * P], m_bt[:, g, b, :], m_xt[:, 2, b, :])
                last.then_inc(S["B"], 1)

            def ssm_c(t):
                pe.wait_ge(S["state"], t + 1)
                pe.wait_ge(S["attn"], t + 1)
                for i in range(2):
                    rows = slice(M2_P * i, M2_P * (i + 1))
                    for b in range(NBLK):
                        out = ps[rows, 4, b * P:(b + 1) * P]
                        mm(out, m_xt[:, 1, b, rows], m_at[:, i, b, :], stop=False)
                        mm(out, m_st[:, b, rows], m_er[:, i, META + b * BLK:META + (b + 1) * BLK], start=False)
                    last = mm(ps[rows, 7, 288:304], m_xtm[0:META, 1, rows], m_atm[0:META, i, :])
                last.then_inc(S["C"], 1)

            def ssm_sum(t):
                pe.wait_ge(S["sq"], t + 1)
                if t == 0:
                    pe.wait_ge(S["state"], M2_T)
                if t == 4:
                    pe.wait_ge(S["r"], 1)
                for a, b in halves(T2):
                    last = mm(pf[:, SSM_SUM + a:SSM_SUM + b], ones[:, :], cv[:, t % 2, a:b],
                              start=(t % 4 == 0), stop=(t % 4 == 3))
                last.then_inc(S["sum"], 1)

            stages = {"norm": norm, "group": group, "prep": prep, "head_a": head_a, "head_b": head_b,
                      "head_c": head_c, "head_d": head_d, "swa_v": lambda _: swa_v(), "swa_a": swa_a,
                      "swa_b": swa_b, "swa_c": swa_c, "ssm_dt": lambda _: ssm_dt(), "ssm_bc": ssm_bc,
                      "ssm_a": ssm_a, "ssm_b": ssm_b, "ssm_c": ssm_c, "ssm_sum": ssm_sum}
            for kind, i in STEPS:
                if kind in stages:
                    stages[kind](i)

        @block.scalar
        def _(act):
            chain = [0]

            table = [None]

            def f(out, in_, func, **k):
                if func in (ACT.Tanh, ACT.Sigmoid, ACT.Silu):
                    table[0] = func
                return nc.scalar.activation(out, in_, func, **k)

            def exp_ln():
                if table[0] != "exp_ln":
                    nc.scalar.preload_act_table_set("natural_log_exp_and_others")
                    table[0] = "exp_ln"

            def link(ins):
                chain[0] += 1
                ins.then_inc(act_chain, 1)
                act.wait_ge(act_chain, chain[0])

            split = [0]

            def split_weights(g):
                until = min(SLABS, (FIRST_UNIT[g + 1] - 1) // PER + AHEAD + 1)
                for s in range(split[0], until):
                    n = min(PER, len(UNITS) - PER * s) * UNIT
                    act.wait_ge(w_in[s % RAW], 16 * (s // RAW + 1))
                    if s >= SPL:
                        act.wait_ge(unit_end, slab_end(s - SPL))
                    f(w_hi[:, s % SPL, 0:n], w_raw[:, s % RAW, 0:n], ACT.Copy).then_inc(w_hi_ok, 1)
                split[0] = max(split[0], until)

            conv_no = [0]

            def group(g):
                split_weights(g)
                kind, i, _ = GROUPS[g]
                free = acc_free[slot_of(g)]
                x = acc(g)
                if kind in ("y", "wo", "down", "oh", "om", "down2", "cx", "cb"):
                    return
                product_done(act, g)
                if kind == "ga":
                    f(ga_sb[0:GLA_RANK, :], x[0:GLA_RANK, :], ACT.Copy).then_inc(free, 1)
                elif kind == "gq":
                    if i:
                        act.wait_ge(ready, i)
                    f(qf1, x, ACT.Copy, scale=float(P) ** -0.5).then_inc(free, 1)
                elif kind == "gk":
                    f(kf1, x, ACT.Copy).then_inc(free, 1)
                elif kind in ("gv", "hi"):
                    n = i if kind == "gv" else GLA_H + i
                    if i:
                        act.wait_ge(st_a, n)
                    f(vf1 if kind == "gv" else vf2, x, ACT.Copy).then_inc(free, 1)
                elif kind in ("gr", "hg"):
                    gate = (g_gate if kind == "gr" else h_gate)[:, i % 2, :]
                    if i >= 2:
                        act.wait_ge(tile_lo, TILE_NO[("y" if kind == "gr" else "v", i - 2)])
                    f(gate, x, ACT.Tanh, scale=0.5).then_inc(act_part, 1)
                elif kind in ("hf", "hq"):
                    act.wait_ge(ready, GLA_H + max(i - 1, 0))
                    if i == 0:
                        act.wait_ge(lb_ok, 1)
                    f((f2 if kind == "hf" else q2)[i % 2], x, ACT.Tanh, scale=0.5).then_inc(act_part, 1)
                elif kind == "sk":
                    act.wait_ge(ready, GLA_H)
                    f(s_k, x, ACT.Copy).then_inc(free, 1)
                elif kind == "sv":
                    f(s_vf, x, ACT.Copy).then_inc(free, 1)
                elif kind == "sq":
                    f(s_q[:, i, :], x, ACT.Copy, scale=float(SWA_HD) ** -0.5).then_inc(free, 1)
                elif kind == "cc":
                    if i == 0:
                        act.wait_ge(tile_lo, TILE_NO[("y", GLA_H - 1)])
                    else:
                        evacuated(act, GROUP_OF[("cx", i - 1)])
                    f(c_c, x, ACT.Copy).then_inc(free, 1)
                elif kind == "gate":
                    m, br = i
                    if 3 * m + br >= 2:
                        evacuated(act, g - 3)
                    elif 3 * m + br == 0:
                        act.wait_ge(tile_lo, TILE_NO[("y", 2 * GLA_H - 1)])
                        act.wait_ge(sw_lo, SWA_G * NBLK)
                    f(mrg[:, 3 * ((3 * m + br) % 2), :], x, ACT.Sigmoid).then_inc(free, 1)
                elif kind in ("up", "up2"):
                    j, half = i
                    c = FT * half + j
                    a = "a" if kind == "up" else "a2"
                    dst = ffn[:, (j % 2) * 2 + half, :]
                    if j >= 2:
                        act.wait_ge(tile_lo, TILE_NO[(a, j - 2)])
                    if kind == "up":
                        f(dst, x, ACT.Identity, scale=pc("fconv", 3 * c + 2)).then_inc(act_part, 1)
                    else:
                        f(dst, x[:, META - USED:], ACT.Identity, scale=pc("fconv2", 3 * c + 2),
                          bias=pc("fconvb2", c)).then_inc(act_part, 1)
                    if half:
                        evacuated(act, g - 1)
                        f(ffn[:, 4 + j % 2, :], ffn[:, (j % 2) * 2, :], ACT.Silu).then_inc(silu_ok, 1)
                elif kind == "dt":
                    act.wait_ge(ready, GLA_H + HG_H)
                    b = pc("dt_bias", rows=M2_H)
                    exp_ln()
                    y = x[0:M2_H, :]
                    f(m_a[0:M2_H, :], pc("a_log", rows=M2_H), ACT.Exp)
                    link(f(sp1[0:M2_H, :], y, ACT.Abs, bias=b))
                    f(dt_t[0:M2_H, :], y, ACT.Relu, bias=b).then_inc(free, 1)
                    link(f(sp1[0:M2_H, :], sp1[0:M2_H, :], ACT.Exp, scale=-1.0))
                    f(sp1[0:M2_H, :], sp1[0:M2_H, :], ACT.Ln, bias=ones[0:M2_H, 0:1]).then_inc(ssm_sem["dt"], 1)
                elif kind in ("mb", "mc", "mx"):
                    c = m2_channel(kind, i)
                    n = conv_no[0]
                    conv_no[0] += 1
                    if n:
                        act.wait_ge(ssm_sem["x"], n)
                    f(cv[:, 0, :], x, ACT.Identity, scale=pc("m2conv", 4 * c + 3), bias=pc("m2convb", c))\
                        .then_inc(act_part, 1)
                    evacuated(act, g)
                    f(cv[:, 1, :], cv[:, 0, :], ACT.Tanh, scale=0.5).then_inc(silu_ok, 1)
                elif kind == "mz":
                    if i >= 2:
                        act.wait_ge(ssm_sem["sum"], i - 1)
                    else:
                        act.wait_ge(ssm_sem["x"], 2 * M2_G + M2_T)
                    f(cv[:, i % 2, :], x, ACT.Tanh, scale=0.5).then_inc(act_part, 1)

            def root(out, x, n):
                link(f(out, x, ACT.Ln, scale=1.0 / n, bias=pc("eps")))
                return f(out, out, ACT.Exp, scale=-0.5)

            def square(which_k):
                which, k = which_k
                i = NORMS.index(which)
                residual_ready(act, which, k)
                c0, c1 = norm_columns(which)
                n = c1 - c0
                if k >= 3:
                    act.wait_ge(sq_added, (KD - 1) * i + k - 2)
                f(full[:, k % 2, 0:n] if k else r_bc[:, 0:n], h_res[:, k, c0:c1], ACT.Square).then_inc(sq_ok, 1)
                if which == "norm1":
                    if k >= 3:
                        act.wait_ge(sq2_added, k - 2)
                    f(ffn[:, 1 + k % 2 if k else 0, :], h_res[:, k, c0:c1], ACT.Square, scale=pc("g_final", k))\
                        .then_inc(sq2_ok, 1)
                    if k == 0:
                        act.wait_ge(meta_in, 16)
                        f(ffn[:, 3, 0:KD * META].rearrange("p (k t) -> p k t", t=META), h_res[:, :, 0:META],
                          ACT.Square).then_inc(meta_sq, 1)

            def norm(which):
                i = NORMS.index(which)
                c0, c1 = norm_columns(which)
                first, n = sums(which)
                if i == 0:
                    split_weights(0)
                exp_ln()
                act.wait_ge(sum_ok, i + 1)
                if i == 0:
                    act.wait_ge(par_in, 48)
                if which == "norm1":
                    r1, t = e2[:, 0, META:T2], e2[:, 1, META:T2]
                    root(r1, pf[:, first:first + n], D).then_inc(first_rstd, 1)
                    f(r_bc[:, 0:META], ps[:, 5, 0:META], ACT.Ln, scale=1.0 / D, bias=pc("eps"))
                    act.wait_ge(scaled_sum, 1)
                    link(f(r_bc[:, META:T2], t, ACT.Ln, scale=1.0 / D, bias=pc("eps")))
                    f(r_bc[:, :], r_bc[:, :], ACT.Exp, scale=-0.5).then_inc(rstd_ok, 1)
                    c0, n = 0, T2
                else:
                    root(r_bc[:, 0:n], pf[:, first:first + n], D).then_inc(rstd_ok, 1)
                if which != "final":
                    for k in range(KD):
                        act.wait_ge(u_full, KD * i + k + 1)
                        f(u_hi[:, k, c0:c1], full[:, k % 2, 0:n], ACT.Copy).then_inc(u_hi_ok, 1)

            def bounds(_):
                act.wait_ge(lbd_ok, 1)
                f(lb, lb, ACT.Exp).then_inc(lbe_ok, 1)

            def prep(n):
                exp_ln()
                if n < GLA_H:
                    act.wait_ge(pa_ok, n + 1)
                    if n == 0:
                        act.wait_ge(negb_ok, 1)
                    x = ps[:, 7, :]
                    link(f(gt1, x, ACT.Abs, bias=pc("b_alpha", n)))
                    link(f(gt1, gt1, ACT.Exp, scale=-1.0))
                    f(gt1, gt1, ACT.Ln, bias=ones[:, 0:1])
                    f(gt2, x, ACT.Relu, scale=-1.0, bias=negb[:, n:n + 1]).then_inc(sp_ok, 1)
                    act.wait_ge(cum_ok, n + 1)
                    s = 1.0 / GLA_TAU
                    f(ge[:, 0, :], ge[:, 0, :], ACT.Exp, scale=-s)
                    f(ge[:, 1, :], ge[:, 1, :], ACT.Exp, scale=s)
                    f(ge[:, 2, :], ge[:, 2, :], ACT.Exp, scale=s)
                    f(ge[:, 3, :], gcum, ACT.Exp, scale=-s).then_inc(exp_ok, 1)
                else:
                    act.wait_ge(f_ok, n - GLA_H + 1)
                    f(lf2, f2[n % 2], ACT.Ln).then_inc(sp_ok, 1)
                    act.wait_ge(cum_ok, n + 1)
                    f(e2[:, 0, :], bc2, ACT.Exp)
                    f(e2[:, 1, :], bc2, ACT.Exp, scale=-1.0)
                    f(e2[:, 2, :], t21, ACT.Exp).then_inc(exp_ok, 1)

            def head_a(n):
                act.wait_ge(st_a, n + 1)
                gla = n < GLA_H
                f(g_ktok if gla else h_ktok, ps[:, 5, :].rearrange("p (b t) -> p b t", t=BLK), ACT.Copy)
                last = f(g_vtok if gla else h_vtok, ps[:, 6, :].rearrange("p (b t) -> p b t", t=BLK), ACT.Copy)
                if not gla:
                    act.wait_ge(attn_ok, n + 1)
                    f(h_ktm[0:META, :], ps[0:META, 7, 16:144], ACT.Copy)
                    last = f(h_vtm[0:META, :], ps[0:META, 7, 144:272], ACT.Copy)
                last.then_inc(tok_ok, 1)

            def head_c(n):
                gla = n < GLA_H
                act.wait_ge(st_c, n + 1)
                if n:
                    act.wait_ge(tile_lo, TILE_NO[("y", n - 1) if n <= GLA_H else ("v", n - 1 - GLA_H)])
                    act.wait_ge(st_d, n)
                if gla:
                    f(g_o, ps[:, 5, :], ACT.Copy)
                    last = f(g_osq, ps[:, 5, :], ACT.Square)
                else:
                    for func, dst in ((ACT.Copy, h_o), (ACT.Square, h_osq)):
                        f(dst[:, META:T2], ps[:, 5, :], func)
                        last = f(dst[:, 0:META], ps[:, 7, 400:416], func)
                last.then_inc(o_ok, 1)

            def head_d(n):
                exp_ln()
                act.wait_ge(st_d, n + 1)
                if n < GLA_H:
                    last = root(g_or, ps[:, 6, :], P)
                else:
                    f(h_or[:, META:T2], ps[:, 6, :], ACT.Ln, scale=1.0 / P, bias=pc("eps"))
                    link(f(h_or[:, 0:META], ps[:, 7, 416:432], ACT.Ln, scale=1.0 / P, bias=pc("eps")))
                    last = f(h_or, h_or, ACT.Exp, scale=-0.5)
                last.then_inc(r_ok, 1)

            def swa_v(_):
                act.wait_ge(sv_t, 1)
                f(s_vtok, ps[:, 4, :].rearrange("p (b t) -> p b t", t=P), ACT.Copy).then_inc(sv_ok, 1)

            def swa_a(n):
                c0 = SWA_W if n < SWA_G else 0
                act.wait_ge(sw_m, n + 1)
                if n:
                    act.wait_ge(sw_t, n)
                else:
                    act.wait_ge(st_c, GLA_H)
                for t in range(SWA_T):
                    f(s_P[:, t, c0:], s_L[:, t, c0:], ACT.Exp, bias=s_small[:, 1, t:t + 1],
                      accum_out=s_small[:, 3, t:t + 1])
                f(s_small[:, 4, :], s_small[:, 2, :], ACT.Exp).then_inc(sw_e, 1)

            def swa_b(n):
                act.wait_ge(sw_t, n + 1)
                j = 1 if n < SWA_G else 0
                if n:
                    act.wait_ge(sw_o, n)
                f(s_PT[:, :, j:, :], pf[:, 6 * BANK:8 * BANK].rearrange("p (t j c) -> p t j c", j=2, c=BLK)[:, :, j:, :],
                  ACT.Copy).then_inc(sw_pt, 1)

            S = ssm_sem

            def ssm_dt(_):
                act.wait_ge(S["turned"], 1)
                f(m_cols, ps[:, 7, 0:128].rearrange("p (a b h) -> p a b h", a=2, b=NBLK), ACT.Copy)
                f(m_colm[0:META], ps[0:META, 7, 128:160].rearrange("p (a h) -> p a h", a=2), ACT.Copy)\
                    .then_inc(S["cols"], 1)

            def ssm_bc(g):
                act.wait_ge(S["bct"], g + 1)
                if g == 0:
                    act.wait_ge(tile_lo, TILE_NO[("v", HG_H - 1)])
                f(m_bt[:, g], ps[:, 4, :].rearrange("p (b t) -> p b t", t=P), ACT.Copy)
                act.wait_ge(S["cb"], g + 1)
                f(m_btm[0:META, g, :], ps[0:META, 7, 0:128], ACT.Copy).then_inc(S["bt"], 1)

            def ssm_a(t):
                act.wait_ge(S["A"], t + 1)
                for i in range(2):
                    f(m_er[:, i, META:T2], ps[:, 4 + i, :], ACT.Exp)
                    ends = ps[:, 4 + i, :].rearrange("p (b t) -> p b t", t=BLK)[:, :, BLK - 1]
                    f(m_al[:, i, :], ends, ACT.Copy)
                    last = f(m_dec[:, i, :], ends, ACT.Exp)
                last.then_inc(S["row"], 1)
                act.wait_ge(S["diff"], t + 1)
                f(m_at, m_at, ACT.Exp)
                f(m_atm[0:META], m_atm[0:META], ACT.Exp)
                f(m_dte, m_dte, ACT.Exp)
                f(m_dtm[0:META, :], m_dtm[0:META, :], ACT.Exp).then_inc(S["exp"], 1)

            def ssm_norm(g):
                exp_ln()
                act.wait_ge(S["sum"], 4 * g + 4)
                act.wait_ge(S["C"], M2_T)
                root(m_er[:, g, :], pf[:, SSM_SUM:SSM_SUM + T2], SEQ).then_inc(S["r"], 1)

            stages = {"square": square, "norm": norm, "bounds": bounds, "group": group, "prep": prep, "head_a": head_a, "head_c": head_c,
                      "head_d": head_d, "swa_v": swa_v, "swa_a": swa_a, "swa_b": swa_b, "ssm_dt": ssm_dt,
                      "ssm_bc": ssm_bc, "ssm_a": ssm_a, "ssm_norm": ssm_norm}
            for kind, i in STEPS:
                if kind in stages:
                    nc.scalar.drain()
                    stages[kind](i)

        @block.vector
        def _(dve):
            chain = [0]
            V = nc.vector
            S = ssm_sem

            def link(ins):
                chain[0] += 1
                ins.then_inc(dve_chain, 1)
                dve.wait_ge(dve_chain, chain[0])

            def tt(out, a, b, op):
                return V.tensor_tensor(out, a, b, op)

            def mul(out, a, b):
                return V.tensor_tensor(out, a, b, ALU.mult)

            def half_mul(out, a, b):
                return V.scalar_tensor_tensor(out=out, in0=a, scalar=0.5, in1=b, op0=ALU.mult, op1=ALU.mult)

            def madd(out, a, s, b):
                return V.scalar_tensor_tensor(out=out, in0=a, scalar=s, in1=b, op0=ALU.mult, op1=ALU.add)

            def twice_silu(out, th, x):
                return V.scalar_tensor_tensor(out=out, in0=th, scalar=1.0, in1=x, op0=ALU.add, op1=ALU.mult)

            def parts(hi, lo, x):
                link(V.tensor_copy(hi, x))
                tt(lo, x, hi, ALU.subtract).then_inc(tile_lo, 1)

            def group(g):
                kind, i, _ = GROUPS[g]
                free = acc_free[slot_of(g)]
                x = acc(g)
                if kind in BOTH:
                    dve.wait_ge(act_part, PART_NO[g])
                elif kind in ("y", "wo", "down", "oh", "om", "down2", "cx", "cb"):
                    product_done(dve, g)
                if kind in ("gr", "hg"):
                    gate = (g_gate if kind == "gr" else h_gate)[:, i % 2, :]
                    twice_silu(gate, gate, x).then_inc(free, 1)
                elif kind == "hf":
                    V.tensor_scalar(f2[i % 2], f2[i % 2], lb1[:, i:i + 1], lb[:, i:i + 1], ALU.mult, ALU.add).then_inc(free, 1)
                    dve.wait_ge(free, TURN[g] + 1)
                    V.tensor_scalar(k2, f2[i % 2], -1.0, 1.0, ALU.mult, ALU.add).then_inc(f_ok, 1)
                elif kind == "hq":
                    twice_silu(q2[i % 2], q2[i % 2], x).then_inc(free, 1)
                elif kind == "cx":
                    evacuated(dve, GROUP_OF[("cc", i)])
                    if i == 0:
                        link(V.memset(c_u[:, 0:2], 0.0))
                    mul(c_u[:, 2:], x, c_c).then_inc(free, 1)
                    dve.wait_ge(free, TURN[g] + 1)
                    link(V.tensor_scalar(c_y, c_u[:, 2:], pc("conv", 3 * i + 2), None, ALU.mult))
                    link(madd(c_y, c_u[:, 1:SEQ + 1], pc("conv", 3 * i + 1), c_y))
                    link(madd(c_y, c_u[:, 0:SEQ], pc("conv", 3 * i), c_y))
                elif kind == "cb":
                    mul(c_a, x, c_y).then_inc(free, 1)
                    dve.wait_ge(free, TURN[g] + 1)
                    parts(y_hi[:, GLA_H + i, :], y_lo[:, GLA_H + i, :], c_a)
                elif kind == "y":
                    m, br = i
                    evacuated(dve, g - 1)
                    gate = mrg[:, 3 * ((3 * m + br) % 2), :]
                    mul(mrg[:, 2 if br else 1, :], x, gate).then_inc(free, 1)
                    dve.wait_ge(free, TURN[g] + 1)
                    if br:
                        link(tt(mrg[:, 1, :], mrg[:, 1, :], mrg[:, 2, :], ALU.add))
                    if br == 2:
                        parts(m_hi[:, m, :], m_lo[:, m, :], mrg[:, 1, :])
                elif kind in ("wo", "down", "oh", "om", "down2"):
                    c0, c1 = columns(g)
                    tile = h_res[:, i, c0:c1]
                    tt(tile, x, tile, ALU.add).then_inc(free, 1)
                elif kind in ("up", "up2"):
                    j, half = i
                    c = FT * half + j
                    dst = ffn[:, (j % 2) * 2 + half, :]
                    if kind == "up":
                        link(madd(dst[:, 1:], x[:, 0:SEQ - 1], pc("fconv", 3 * c + 1), dst[:, 1:]))
                        madd(dst[:, 2:], x[:, 0:SEQ - 2], pc("fconv", 3 * c), dst[:, 2:]).then_inc(free, 1)
                    else:
                        o = META - USED
                        link(madd(dst, x[:, o - 1:o - 1 + SEQ], pc("fconv2", 3 * c + 1), dst))
                        madd(dst, x[:, o - 2:o - 2 + SEQ], pc("fconv2", 3 * c), dst).then_inc(free, 1)
                    if half:
                        dve.wait_ge(free, TURN[g] + 1)
                        dve.wait_ge(silu_ok, j + 1 + (0 if kind == "up" else FT + M2_T + 2 * M2_G))
                        link(mul(ffn[:, 6, :], ffn[:, 4 + j % 2, :], dst))
                        parts(a_hi[:, j, :], a_lo[:, j, :], ffn[:, 6, :])
                elif kind == "dt":
                    dve.wait_ge(S["dt"], 1)
                    r = slice(0, M2_H)
                    V.tensor_scalar(m_a[r, :], m_a[r, :], -1.0, None, ALU.mult)
                    link(tt(dt_t[r, :], dt_t[r, :], sp1[r, :], ALU.add))
                    link(V.tensor_scalar(sp2[r, :], dt_t[r, :], m_a[r, 0:1], None, ALU.mult))
                    V.tensor_tensor_scan(ac_t[r, :], seg128[r, :], sp2[r, :], 0.0, ALU.mult, ALU.add)\
                        .then_inc(S["cum"], 1)
                elif kind in ("mb", "mc", "mx"):
                    c = m2_channel(kind, i)
                    dst = cv[:, 0, :]
                    link(madd(dst[:, 1:], x[:, 0:T2 - 1], pc("m2conv", 4 * c + 2), dst[:, 1:]))
                    link(madd(dst[:, 2:], x[:, 0:T2 - 2], pc("m2conv", 4 * c + 1), dst[:, 2:]))
                    madd(dst[:, 3:], x[:, 0:T2 - 3], pc("m2conv", 4 * c), dst[:, 3:]).then_inc(free, 1)
                    dve.wait_ge(silu_ok, FT + {"mb": 0, "mc": M2_G, "mx": 2 * M2_G}[kind] + i + 1)
                    out = {"mb": m_bc[:, i % 2, :], "mc": m_bc[:, 2 + i % 2, :], "mx": m_x[:, i % 2, :]}[kind]
                    link(twice_silu(out, cv[:, 1, :], dst))
                    V.tensor_scalar(out, out, 0.5, None, ALU.mult).then_inc(S["x"], 1)
                elif kind == "mz":
                    z = cv[:, i % 2, :]
                    twice_silu(z, z, x).then_inc(free, 1)
                    dve.wait_ge(free, TURN[g] + 1)
                    link(half_mul(m_y[:, i, :], m_y[:, i, :], z))
                    mul(z, m_y[:, i, :], m_y[:, i, :]).then_inc(S["sq"], 1)

            def square(which_k):
                which, k = which_k
                i = NORMS.index(which)
                c0, c1 = norm_columns(which)
                n = c1 - c0
                if (which, k) == ("g_mix", 0):
                    V.memset(ones[:, :], 1.0).then_inc(zeroed, 1)
                if k:
                    dve.wait_ge(sq_ok, KD * i + k + 1)
                    tt(r_bc[:, 0:n], r_bc[:, 0:n], full[:, k % 2, 0:n], ALU.add).then_inc(sq_added, 1)
                if which == "norm1" and k:
                    dve.wait_ge(sq2_ok, k + 1)
                    tt(ffn[:, 0, :], ffn[:, 0, :], ffn[:, 1 + k % 2, :], ALU.add).then_inc(sq2_added, 1)
                if which == "norm1" and k == 0:
                    dve.wait_ge(meta_sq, 1)
                    V.tensor_reduce(ffn[:, 4, 0:META], ffn[:, 3, 0:KD * META].rearrange("p (k t) -> p t k", t=META),
                                    AXX, ALU.add).then_inc(meta_sum, 1)
                    mul(gain1[:, :], par[:, PCOL["g_final"]:PCOL["g_final"] + KD],
                        par[:, PCOL["norm1"]:PCOL["norm1"] + KD])

            def norm(which):
                i = NORMS.index(which)
                if i == 0:
                    dve.wait_ge(par_in, 48)
                c0, c1 = norm_columns(which)
                n = c1 - c0
                two = which == "norm1"
                if two:
                    r1, t = e2[:, 0, META:T2], e2[:, 1, META:T2]
                    dve.wait_ge(first_rstd, 1)
                    link(mul(t, ps[:, 6, :], r1))
                    mul(t, t, r1).then_inc(scaled_sum, 1)
                    dve.wait_ge(rstd_ok, i + 1)
                    link(mul(r_bc[:, META:T2], r_bc[:, META:T2], r1))
                    c0, n = 0, T2
                dve.wait_ge(rstd_ok, i + 1)

                def scaled(out, k, g, cols, r):
                    return V.scalar_tensor_tensor(out=out, in0=h_res[:, k, cols], scalar=g, in1=r,
                                                  op0=ALU.mult, op1=ALU.mult)

                def gain(k):
                    if two:
                        scaled(full[:, k % 2, 0:META], k, pc("norm1", k), slice(0, META), r_bc[:, 0:META])
                        return scaled(full[:, k % 2, META:T2], k, gain1[:, k:k + 1], slice(META, T2), r_bc[:, META:T2])
                    return scaled(full[:, k % 2, 0:n], k, pc(which, k), slice(c0, c1), r_bc[:, 0:n])

                def low(k):
                    dve.wait_ge(u_hi_ok, KD * i + k + 1)
                    tt(u_lo[:, k, c0:c1], full[:, k % 2, 0:n], u_hi[:, k, c0:c1], ALU.subtract)\
                        .then_inc(u_lo_ok, 1)

                if which == "final":
                    for k in range(KD):
                        scaled(h_res[:, k, c0:c1], k, pc(which, k), slice(c0, c1), r_bc[:, 0:n]).then_inc(out_ok, 1)
                    return
                for k in range(KD):
                    if k >= 2:
                        dve.wait_ge(u_lo_ok, KD * i + k - 1)
                    gain(k).then_inc(u_full, 1)
                    if k:
                        low(k - 1)
                low(KD - 1)
                if which == "g_mix":
                    V.memset(g_attn, 0.0)
                    link(V.tensor_scalar(negb, par[:, PCOL["b_alpha"]:PCOL["b_alpha"] + GLA_H], -1.0, None, ALU.mult))
                    V.memset(s_small[:, 7, 0:1], 0.0).then_inc(negb_ok, 1)

            def bounds(_):
                a, b = PCOL["lb0"], PCOL["lb1"]
                tt(lb, par[:, b:b + HG_H], par[:, a:a + HG_H], ALU.subtract).then_inc(lbd_ok, 1)
                dve.wait_ge(lbe_ok, 1)
                link(V.tensor_scalar(lb, lb, 1.0, None, ALU.add))
                link(V.reciprocal(lb, lb))
                link(V.tensor_scalar(lb1, lb, -0.5, 0.5, ALU.mult, ALU.add))
                tt(lb, lb, lb1, ALU.add).then_inc(lb_ok, 1)

            def second_start(part):
                if part == 0:
                    for k in range(KD):
                        V.scalar_tensor_tensor(out=h_res[:, k, META:T2], in0=h_res[:, k, META:T2],
                                               scalar=pc("g_final", k), in1=e2[:, 0, META:T2],
                                               op0=ALU.mult, op1=ALU.mult)
                else:
                    V.memset(KC, 0.0)
                    V.memset(h_attn, 0.0)
                    V.memset(h_am, 0.0)
                    V.memset(dshift, 0.0)

            def bc(v, n):
                return v.unsqueeze(len(v.shape)).broadcast_to(tuple(v.shape) + (n,))

            def prep(n):
                if n < GLA_H:
                    dve.wait_ge(sp_ok, n + 1)
                    link(tt(gt1, gt1, gt2, ALU.add))
                    link(V.tensor_tensor_scan(gcum, seg64, gt1, 0.0, ALU.mult, ALU.add))
                    cum = gcum.rearrange("p (c t) -> p c t", t=GLA_C)
                    e = [ge[:, j, :].rearrange("p (c t) -> p c t", t=GLA_C) for j in range(4)]
                    tt(e[0], cum, bc(cum[:, :, GLA_C // 2 - 1], GLA_C), ALU.subtract)
                    tt(e[1], cum, bc(cum[:, :, GLA_C // 2 - 1], GLA_C), ALU.subtract)
                    tt(e[2], cum, bc(cum[:, :, GLA_C - 1], GLA_C), ALU.subtract).then_inc(cum_ok, 1)
                    dve.wait_ge(exp_ok, n + 1)
                    evacuated(dve, GROUP_OF[("gq", n)])
                    evacuated(dve, GROUP_OF[("gk", n)])
                    if n:
                        dve.wait_ge(st_c, n)
                    v = "p (b c t) -> p b c t"
                    q4, k4 = qf1.rearrange(v, c=2, t=GLA_C), kf1.rearrange(v, c=2, t=GLA_C)
                    eL, eB = ge[:, 2, :].rearrange(v, c=2, t=GLA_C), ge[:, 3, :].rearrange(v, c=2, t=GLA_C)
                    d = eB[:, :, :, GLA_C - 1]
                    mul(g_qE, qf1, ge[:, 0, :])
                    mul(g_kE, kf1, ge[:, 1, :])
                    mul(g_kL, k4[:, :, 0, :], eL[:, :, 0, :])
                    mul(g_kZ[:, :, GLA_C:], k4[:, :, 1, :], eL[:, :, 1, :])
                    mul(g_qZ[:, :, 0:GLA_C], q4[:, :, 0, :], eB[:, :, 0, :])
                    mul(g_D, d[:, :, 0], d[:, :, 1])
                    link(mul(g_qB, q4[:, :, 1, :], eB[:, :, 1, :]))
                    mul(g_kZ[:, :, 0:GLA_C], g_kL, bc(d[:, :, 1], GLA_C))
                    mul(g_qZ[:, :, GLA_C:], g_qB, bc(d[:, :, 0], GLA_C)).then_inc(ready, 1)
                    return
                dve.wait_ge(sp_ok, n + 1)
                link(V.tensor_tensor_scan(bc2, seg16, lf2, 0.0, ALU.mult, ALU.add))
                cum = bc2.rearrange("p (c t) -> p c t", t=HG_C)
                tt(t21.rearrange("p (c t) -> p c t", t=HG_C), bc(cum[:, :, HG_C - 1], HG_C), cum, ALU.subtract)\
                    .then_inc(cum_ok, 1)
                dve.wait_ge(exp_ok, n + 1)
                dve.wait_ge(st_c, n)
                kc = KC.rearrange("p b (c t) -> p b c t", t=BLK + HG_C)

                def sub(v):
                    return v[:, META:T2].rearrange("p (b c t) -> p b c t", c=SUB, t=HG_C)

                dec = sub(e2[:, 0, :])[:, :, :, HG_C - 1]
                half_mul(qd2, q2[n % 2], e2[:, 0, :])
                mul(kcm[:, 0, :], k2[:, 0:META], e2[:, 1, 0:META])
                mul(kcm[:, 1, :], k2[:, 0:META], e2[:, 2, 0:META])
                for b in range(NBLK):
                    mul(kc[:, b, :, 0:HG_C], sub(k2)[:, b], sub(e2[:, 1, :])[:, b])
                    mul(kc[:, b, :, BLK:], sub(k2)[:, b], sub(e2[:, 2, :])[:, b])
                ds8 = dshift.rearrange("p (b c) -> p b c", c=SUB)
                dc8 = dcum.rearrange("p (b c) -> p b c", c=SUB)
                link(V.tensor_copy(ds8[:, :, 1:], dec[:, :, 0:SUB - 1]))
                link(V.tensor_tensor_scan(dcum, dshift, first8, 0.0, ALU.mult, ALU.add))
                mul(h_D, dc8[:, :, SUB - 1], dec[:, :, SUB - 1])
                mul(qz2.rearrange("p b t -> p (b t)").rearrange("p (c t) -> p c t", t=HG_C),
                    qd2[:, META:T2].rearrange("p (c t) -> p c t", t=HG_C), bc(dcum, HG_C))
                for c in range(1, SUB):
                    last = mul(KC[:, :, (c + 1) * BLK:(c + 1) * BLK + HG_C * c], KC[:, :, c * BLK:c * BLK + HG_C * c],
                               bc(dec[:, :, c], HG_C * c))
                    if c < SUB - 1:
                        link(last)
                last.then_inc(ready, 1)

            def head_a(n):
                gla = n < GLA_H
                dve.wait_ge(st_a, n + 1)
                m4 = msk[:, :].unsqueeze(1).broadcast_to((P, NBLK, BLK))
                last = V.copy_predicated(g_attn if gla else h_attn, m4,
                                         ps[:, 4, :].rearrange("p (b t) -> p b t", t=BLK))
                if not gla:
                    last = V.copy_predicated(h_am[0:META, :], msk[0:META, 0:META], ps[0:META, 7, 0:16])
                last.then_inc(attn_ok, 1)

            def head_b(n):
                gla = n < GLA_H
                dve.wait_ge(st_b, n + 1)
                st, dd = (g_state, g_D) if gla else (h_state, h_D)
                if gla:
                    link(V.tensor_copy(st[:, 1, :], ps[:, 4, 0:BLK]))
                else:
                    link(V.tensor_copy(st[:, 0, :], ps[:, 7, 272:400]))
                first = 1 if gla else 0
                for b in range(first, NBLK - 1):
                    last = madd(st[:, b + 1, :], st[:, b, :], dd[:, b:b + 1], ps[:, 4, b * BLK:(b + 1) * BLK])
                    if b < NBLK - 2:
                        link(last)
                last.then_inc(state_ok, 1)

            def head_d(n):
                gla = n < GLA_H
                dve.wait_ge(r_ok, n + 1)
                i = n if gla else n - GLA_H
                o, r, gate = (g_o, g_or, g_gate) if gla else (h_o, h_or, h_gate)
                hi, lo = (y_hi, y_lo) if gla else (v_hi, v_lo)
                link(V.scalar_tensor_tensor(out=o, in0=o, scalar=pc("gla_norm" if gla else "hg_norm", i), in1=r,
                                            op0=ALU.mult, op1=ALU.mult))
                link(half_mul(o, o, gate[:, i % 2, :]))
                parts(hi[:, i, :], lo[:, i, :], o)

            def swa_a(n):
                b, g = n // SWA_G, n % SWA_G
                c0 = SWA_W if b == 0 else 0
                dve.wait_ge(sw_s, n + 1)
                for t in range(SWA_T):
                    slope = 2.0 ** -(SWA_T * g + t + 1)
                    last = madd(s_L[:, t, c0:], dist[:, c0:], slope, pf[:, 4 * BANK + 256 * t + c0:4 * BANK + 256 * (t + 1)])
                link(last)
                link(V.tensor_reduce(s_small[:, 0, :], s_L[:, :, c0:], AXX, ALU.max))
                sink = par[:, PCOL["sinks"] + SWA_T * g:PCOL["sinks"] + SWA_T * (g + 1)]
                link(tt(s_small[:, 0, :], s_small[:, 0, :], sink, ALU.max))
                V.tensor_scalar(s_small[:, 1, :], s_small[:, 0, :], -1.0, None, ALU.mult)
                tt(s_small[:, 2, :], sink, s_small[:, 0, :], ALU.subtract).then_inc(sw_m, 1)
                dve.wait_ge(sw_e, n + 1)
                link(tt(s_small[:, 5, :], s_small[:, 3, :], s_small[:, 4, :], ALU.add))
                link(V.reciprocal(s_small[:, 5, :], s_small[:, 5, :]))
                mul(s_P[:, :, c0:], s_P[:, :, c0:], bc(s_small[:, 5, :], 256 - c0)).then_inc(sw_p, 1)

            def swa_c(n):
                b, g = n // SWA_G, n % SWA_G
                rows = slice(SWA_HD * g, SWA_HD * (g + 1))
                dve.wait_ge(sw_o, n + 1)
                x = ps[rows, 3, :].rearrange("p (t c) -> p t c", c=BLK)
                hi = y_hi[rows, 8:12, b * BLK:(b + 1) * BLK]
                link(V.tensor_copy(hi, x))
                tt(y_lo[rows, 8:12, b * BLK:(b + 1) * BLK], x, hi, ALU.subtract).then_inc(sw_lo, 1)

            def ssm_dt(_):
                V.memset(m_cb, 0.0)
                link(V.memset(m_cbm, 0.0))

            def ssm_bc(g):
                dve.wait_ge(S["bct"], g + 1)
                m4 = msk[:, :].unsqueeze(1).broadcast_to((P, NBLK, BLK))
                V.copy_predicated(m_cb[:, g], m4, ps[:, 5, :].rearrange("p (b t) -> p b t", t=BLK))
                V.copy_predicated(m_cbm[0:META, g, :], msk[0:META, 0:META], ps[0:META, 7, 128:144])\
                    .then_inc(S["cb"], 1)

            def ssm_a(t):
                g, h0 = t // 4, 2 * t
                rm = slice(0, META)
                dve.wait_ge(S["A"], t + 1)
                dve.wait_ge(S["cols"], 1)
                dve.wait_ge(S["row"], t + 1)
                for i in range(2):
                    for b in range(NBLK):
                        V.tensor_scalar(m_at[:, i, b, :], ps[:, 4 + i, b * BLK:(b + 1) * BLK],
                                        m_cols[:, 0, b, h0 + i:h0 + i + 1], 0.0, ALU.subtract, ALU.min)
                    V.tensor_scalar(m_atm[rm, i, :], ps[rm, 7, 16 * i:16 * i + 16], m_colm[rm, 0, h0 + i:h0 + i + 1],
                                    0.0, ALU.subtract, ALU.min)
                    tt(m_dtm[rm, i:i + 1], ps[rm, 7, 16 * i + 15:16 * i + 16], m_colm[rm, 0, h0 + i:h0 + i + 1],
                       ALU.subtract)
                tt(m_dte, m_al, m_cols[:, 0, :, h0:h0 + 2].rearrange("p b i -> p i b"), ALU.subtract)\
                    .then_inc(S["diff"], 1)
                for i in range(2):
                    mul(m_er[:, i, META:T2], m_er[:, i, META:T2], m_bc[:, 2 + g, META:T2])
                xt = ps[:, 6, :].rearrange("p (b i d) -> p b i d", b=NBLK, i=2)
                xtm = ps[rm, 7, 32:160].rearrange("p (i d) -> p i d", i=2)
                split = "p b (i d) -> p b i d"
                mul(m_xt[:, 1].rearrange(split, i=2), xt, bc(m_cols[:, 1, :, h0:h0 + 2], M2_P))
                mul(m_xtm[rm, 1, :].rearrange("p (i d) -> p i d", i=2), xtm, bc(m_colm[rm, 1, h0:h0 + 2], M2_P))
                dve.wait_ge(S["exp"], t + 1)
                mul(m_dte, m_dte, m_cols[:, 1, :, h0:h0 + 2].rearrange("p b i -> p i b"))
                link(mul(m_dtm[rm, :], m_dtm[rm, :], m_colm[rm, 1, h0:h0 + 2]))
                mul(m_xt[:, 2].rearrange(split, i=2), xt, bc(m_dte.rearrange("p i b -> p b i"), M2_P))
                mul(m_xtm[rm, 2, :].rearrange("p (i d) -> p i d", i=2), xtm, bc(m_dtm[rm, :], M2_P))\
                    .then_inc(S["xt"], 1)
                for i in range(2):
                    mul(m_at[:, i], m_at[:, i], m_cb[:, g])
                    last = mul(m_atm[rm, i, :], m_atm[rm, i, :], m_cbm[rm, g, :])
                last.then_inc(S["attn"], 1)

            def ssm_b(t):
                dve.wait_ge(S["B"], t + 1)
                link(V.tensor_copy(m_st[:, 0, :], ps[:, 7, 160:288]))
                for b in range(NBLK - 1):
                    for i in range(2):
                        c = slice(M2_P * i, M2_P * (i + 1))
                        last = madd(m_st[:, b + 1, c], m_st[:, b, c], m_dec[:, i, b:b + 1],
                                    ps[:, 6, b * P + M2_P * i:b * P + M2_P * (i + 1)])
                    if b < NBLK - 2:
                        link(last)
                last.then_inc(S["state"], 1)

            def ssm_c(t):
                dve.wait_ge(S["C"], t + 1)
                madd(m_y[:, t, META:T2], m_x[:, t % 2, META:T2], pc("m2d", t), ps[:, 4, :])
                madd(m_y[:, t, 0:META], m_x[:, t % 2, 0:META], pc("m2d", t), ps[:, 7, 288:304]).then_inc(S["y"], 1)

            def ssm_norm(g):
                dve.wait_ge(S["r"], g + 1)
                product_done(dve, GROUP_OF[("oh", KD - 1)])
                for t in range(4 * g, 4 * g + 4):
                    y = m_y[:, t, :]
                    link(V.scalar_tensor_tensor(out=y, in0=y, scalar=pc("m2norm", t), in1=m_er[:, g, :],
                                                op0=ALU.mult, op1=ALU.mult))
                    parts(v_hi[:, t, :], v_lo[:, t, :], y)

            stages = {"square": square, "norm": norm, "bounds": bounds, "second_start": second_start, "group": group, "prep": prep, "head_a": head_a, "head_b": head_b,
                      "head_d": head_d, "swa_a": swa_a, "swa_c": swa_c, "ssm_dt": ssm_dt,
                      "ssm_bc": ssm_bc, "ssm_a": ssm_a, "ssm_b": ssm_b, "ssm_c": ssm_c, "ssm_norm": ssm_norm}
            for kind, i in STEPS:
                if kind in stages:
                    V.drain()
                    stages[kind](i)


def constants():
    c = np.zeros((P, 416 + 2 * T2 + SEQ), np.float32)
    c[:, 0:128] = np.eye(P)
    i, j = np.arange(P)[:, None], np.arange(2 * SWA_W)[None, :]
    dist = SWA_W + i - j
    c[:, 128:384] = np.where((dist >= 0) & (dist < SWA_W), -dist, -1e32)
    c[:, 384:416] = (np.arange(32) % SUB == 0)
    t = np.arange(T2)
    c[:, 416:416 + T2] = (t % HG_C != 0)
    c[:, 416 + T2:416 + 2 * T2] = (t >= 1) & ((t < META) | ((t - META) % BLK != 0))
    c[:, 416 + 2 * T2:] = (np.arange(SEQ) % GLA_C != 0)
    mask = (np.arange(P)[:, None] <= np.arange(P)[None, :]).astype(np.int32)
    return c, mask


def lay_out(a):
    def rows_of(name, k):
        if name == "w_swa_o":
            return np.r_[k * SWA_HD:(k + 1) * SWA_HD, (k + SWA_T) * SWA_HD:(k + SWA_T + 1) * SWA_HD]
        return slice(k * P, (k + 1) * P)

    def cols_of(col):
        if isinstance(col, tuple):
            return np.r_[col[0]:col[0] + SWA_HD, col[1]:col[1] + SWA_HD]
        return slice(col, col + P)

    w = np.zeros((SLABS, P, PER * UNIT), np.float32)
    for u, (name, k, col, _, _) in enumerate(UNITS):
        m = a[name][0][rows_of(name, k), cols_of(col)]
        if name == "w_in" and col == 2048:
            m = m[:, 0:GLA_RANK]
        w[u // PER, :, UNIT * (u % PER):UNIT * (u % PER) + m.shape[1]] = m

    p = np.zeros((P, NPAR), np.float32)

    def put(name, v):
        p[:, PCOL[name]:PCOL[name] + v.shape[1]] = v

    def tiles(v):
        return v.reshape(-1, P).T

    def taps(v):
        return v.reshape(v.shape[0], -1, P).transpose(2, 1, 0).reshape(P, -1)

    for name, v in (("g_mix", a["g_mix"][0]), ("g_ffn", a["g_ffn"][0]), ("b_alpha", a["gla_b_alpha"][0]),
                    ("gla_norm", a["gla_norm_g"][0]), ("norm1", a["norm1_w_2"][0]), ("lb0", a["hg_lb_logits_2"][0]),
                    ("lb1", a["hg_lb_logits_2"][1]), ("hg_norm", a["hg_norm_w_2"][0]),
                    ("m2convb", a["m2_conv_b_2"][0]), ("m2norm", a["m2_norm_w_2"][0]), ("norm2", a["norm2_w_2"][0]),
                    ("fconvb2", a["ffn_conv_b_2"][0]), ("final", a["final_norm_w_2"]),
                    ("m2d", np.repeat(a["m2_d_2"][0], M2_P))):
        put(name, tiles(v))
    put("g_final", tiles(a["g_final"]))
    put("conv", taps(a["conv_w"][0]))
    put("fconv", taps(a["ffn_conv_w"][0]))
    put("m2conv", taps(a["m2_conv_w_2"][0]))
    put("fconv2", taps(a["ffn_conv_w_2"][0]))
    put("sinks", np.broadcast_to(a["swa_sinks"][0][None, :], (P, 8)))
    p[0:M2_H, PCOL["dt_bias"]] = a["m2_dt_bias_2"][0]
    p[0:M2_H, PCOL["a_log"]] = a["m2_a_log_2"][0]
    p[:, PCOL["eps"]] = EPS
    c, mask = constants()
    return {"weights": w, "xT": np.ascontiguousarray(a["x"][0].T), "metaT": np.ascontiguousarray(a["meta_tokens_2"].T),
            "params": p, "consts": c, "cmask": mask, "w_alpha": np.ascontiguousarray(a["gla_w_alpha"][0])}


def kernel(**inputs):
    import concourse.bacc as bacc
    from concourse.bass_utils import run_bass_kernel_spmd

    arrays = lay_out({k: np.asarray(v) for k, v in inputs.items()})
    nc = bacc.Bacc("TRN2", target_bir_lowering=False, num_devices=1)
    args = [nc.dram_tensor(k, v.shape, mybir.dt.from_np(v.dtype), kind="ExternalInput").ap()
            for k, v in arrays.items()]
    out = nc.dram_tensor("outT", (D, SEQ), F32, kind="ExternalOutput").ap()
    program(nc, *args, out)
    r = run_bass_kernel_spmd(nc, [arrays], core_ids=[0])
    return np.ascontiguousarray(r.results[0]["outT"].T)[None]
```
